# Optimizing a Trainium2 kernel written in Bass

```python
import math
import jax, jax.numpy as jnp
from jax import lax
import numpy as np

D_MODEL = 1024
BATCH = 1
SEQ = 512
DEPTH = 2

BRANCH_WIDTH = 512
N_BRANCHES = 3
SWA_Q_HEADS = 8
SWA_KV_HEADS = 2
SWA_GROUP = SWA_Q_HEADS // SWA_KV_HEADS
SWA_HEAD_DIM = BRANCH_WIDTH // SWA_Q_HEADS
WINDOW = 128
N_BUCKETS = 32
MAX_DISTANCE = 128
CONV_CHANNELS = BRANCH_WIDTH
CONV_WIDTH = 31
MLA_HEADS = 8
MLA_Q_RANK = 256
MLA_KV_RANK = 128
MLA_NOPE_DIM = 64
MLA_ROPE_DIM = 32
MLA_V_DIM = BRANCH_WIDTH // MLA_HEADS
ROPE_THETA = 10000.0
Q_BLOCK = 128
D_FF = 4 * D_MODEL
EPS = 1e-6
NEG_INF = -1e30

IN_SPLIT_SIZES = (
    SWA_Q_HEADS * SWA_HEAD_DIM,
    SWA_KV_HEADS * SWA_HEAD_DIM,
    SWA_KV_HEADS * SWA_HEAD_DIM,
    2 * CONV_CHANNELS,
    MLA_Q_RANK,
    MLA_KV_RANK,
    MLA_ROPE_DIM,
    N_BRANCHES * D_MODEL,
)
IN_COLS = sum(IN_SPLIT_SIZES)
IN_SPLIT_POINTS = tuple(sum(IN_SPLIT_SIZES[: i + 1]) for i in range(len(IN_SPLIT_SIZES) - 1))


def rms_norm(x, g):
    xf = x.astype(jnp.float32)
    y = xf * lax.rsqrt(jnp.mean(xf * xf, axis=-1, keepdims=True) + EPS)
    return (y * g.astype(jnp.float32)).astype(x.dtype)

def layer_norm(x, g, b):
    xf = x.astype(jnp.float32)
    mu = jnp.mean(xf, axis=-1, keepdims=True)
    var = jnp.mean(jnp.square(xf - mu), axis=-1, keepdims=True)
    y = (xf - mu) * lax.rsqrt(var + EPS) * g.astype(jnp.float32) + b.astype(jnp.float32)
    return y.astype(x.dtype)

def t5_bucket(rel):
    n = jnp.maximum(rel, 0)
    max_exact = N_BUCKETS // 2
    nf = jnp.maximum(n, max_exact).astype(jnp.float32)
    large = max_exact + (jnp.log(nf / max_exact) / math.log(MAX_DISTANCE / max_exact)
                         * (N_BUCKETS - max_exact)).astype(jnp.int32)
    return jnp.where(n < max_exact, n, jnp.minimum(large, N_BUCKETS - 1))

def band_frames(t):
    b, s = t.shape[:2]
    blocks = t.reshape((b, s // WINDOW, WINDOW) + t.shape[2:])
    prev = jnp.concatenate([jnp.zeros_like(blocks[:, :1]), blocks[:, :-1]], axis=1)
    return jnp.concatenate([prev, blocks], axis=2)

def swa_bias_and_mask(positions, rel_bias):
    b, s = positions.shape
    nb = s // WINDOW
    pq = positions.reshape(b, nb, WINDOW)
    pk = band_frames(positions)
    bucket = t5_bucket(pq[..., :, None] - pk[..., None, :])
    bias = rel_bias[bucket].astype(jnp.float32).reshape(b, nb, WINDOW, 2 * WINDOW, SWA_KV_HEADS, SWA_GROUP)
    qi = WINDOW + jnp.arange(WINDOW)[:, None]
    ki = jnp.arange(2 * WINDOW)[None, :]
    in_band = (ki <= qi) & (qi - ki < WINDOW)
    has_prev = (jnp.arange(nb) > 0)[:, None, None] | (ki >= WINDOW)[None]
    mask = in_band[None] & has_prev
    return bias, mask[None, :, :, :, None, None]

def swa_attention(q, k, v, sinks, bias, mask):
    b, s = q.shape[:2]
    nb = s // WINDOW
    qb = q.reshape(b, nb, WINDOW, SWA_KV_HEADS, SWA_GROUP, SWA_HEAD_DIM)
    kk = band_frames(k.reshape(b, s, SWA_KV_HEADS, SWA_HEAD_DIM))
    vv = band_frames(v.reshape(b, s, SWA_KV_HEADS, SWA_HEAD_DIM))
    scores = jnp.einsum('bnqhgd,bnkhd->bnqkhg', qb, kk).astype(jnp.float32) * (SWA_HEAD_DIM ** -0.5) + bias
    scores = jnp.where(mask, scores, NEG_INF)
    sink = sinks.astype(jnp.float32).reshape(SWA_KV_HEADS, SWA_GROUP)
    m = jnp.maximum(scores.max(axis=3, keepdims=True), sink)
    p = jnp.exp(scores - m)
    p = p / (p.sum(axis=3, keepdims=True) + jnp.exp(sink - m))
    out = jnp.einsum('bnqkhg,bnkhd->bnqhgd', p.astype(vv.dtype), vv)
    return out.reshape(b, s, SWA_Q_HEADS * SWA_HEAD_DIM)

def conformer_conv(u_glu, w_dw, b_dw, g_ln, b_ln):
    a, gate = jnp.split(u_glu, 2, axis=-1)
    u = a * jax.nn.sigmoid(gate)
    u = lax.conv_general_dilated(u, w_dw, window_strides=(1,), padding=[(CONV_WIDTH - 1, 0)],
                                 dimension_numbers=('NWC', 'WIO', 'NWC'),
                                 feature_group_count=CONV_CHANNELS) + b_dw
    return jax.nn.silu(layer_norm(u, g_ln, b_ln))

def rope(x, positions):
    d = x.shape[-1]
    half = d // 2
    freqs = jnp.exp(-math.log(ROPE_THETA) * jnp.arange(half, dtype=jnp.float32) / half)
    ang = positions.astype(jnp.float32)[..., None] * freqs
    cos = jnp.cos(ang)[:, :, None, :]
    sin = jnp.sin(ang)[:, :, None, :]
    x1 = x[..., :half].astype(jnp.float32)
    x2 = x[..., half:].astype(jnp.float32)
    return jnp.concatenate([x1 * cos - x2 * sin, x2 * cos + x1 * sin], axis=-1).astype(x.dtype)

def mla_attention(cq, ckv, kpe_raw, positions, g_qn, w_uq, g_kvn, w_ukv):
    b, s = cq.shape[:2]
    q = (rms_norm(cq, g_qn) @ w_uq).reshape(b, s, MLA_HEADS, MLA_NOPE_DIM + MLA_ROPE_DIM)
    q_nope = q[..., :MLA_NOPE_DIM]
    q_pe = rope(q[..., MLA_NOPE_DIM:], positions)
    kv = (rms_norm(ckv, g_kvn) @ w_ukv).reshape(b, s, MLA_HEADS, MLA_NOPE_DIM + MLA_V_DIM)
    k_nope = kv[..., :MLA_NOPE_DIM]
    v = kv[..., MLA_NOPE_DIM:]
    k_pe = rope(kpe_raw[:, :, None, :], positions)[:, :, 0]
    scale = (MLA_NOPE_DIM + MLA_ROPE_DIM) ** -0.5
    nb = s // Q_BLOCK
    key_idx = jnp.arange(s)

    def to_blocks(t):
        return jnp.moveaxis(t.reshape((b, nb, Q_BLOCK) + t.shape[2:]), 1, 0)

    def attend_block(args):
        qn, qp, blk = args
        sc = (jnp.einsum('bqhd,bkhd->bhqk', qn, k_nope)
              + jnp.einsum('bqhd,bkd->bhqk', qp, k_pe)).astype(jnp.float32) * scale
        q_idx = blk * Q_BLOCK + jnp.arange(Q_BLOCK)
        sc = jnp.where(key_idx[None, :] <= q_idx[:, None], sc, NEG_INF)
        p = jax.nn.softmax(sc, axis=-1)
        return jnp.einsum('bhqk,bkhd->bqhd', p.astype(v.dtype), v)

    out = lax.map(attend_block, (to_blocks(q_nope), to_blocks(q_pe), jnp.arange(nb)))
    return jnp.moveaxis(out, 0, 1).reshape(b, s, MLA_HEADS * MLA_V_DIM)

def first_inputs(seed: int = 0) -> dict:
    key = jax.random.key(seed)
    ks = jax.random.split(key, 20)
    f32 = jnp.float32

    def nrm(k, shape, scale):
        return jax.random.normal(k, shape, f32) * scale

    def gain(k, shape):
        return 1.0 + 0.05 * jax.random.normal(k, shape, f32)

    return {
        "x": nrm(ks[0], (BATCH, SEQ, D_MODEL), 1.0),
        "positions": jnp.broadcast_to(jnp.arange(SEQ, dtype=jnp.int32), (BATCH, SEQ)),
        "rel_bias": nrm(ks[1], (N_BUCKETS, SWA_Q_HEADS), 0.5),
        "g_final": gain(ks[2], (D_MODEL,)),
        "g_mix": gain(ks[3], (DEPTH, D_MODEL)),
        "w_in": nrm(ks[4], (DEPTH, D_MODEL, IN_COLS), D_MODEL ** -0.5),
        "swa_sinks": nrm(ks[5], (DEPTH, SWA_Q_HEADS), 0.5),
        "g_q_norm": gain(ks[6], (DEPTH, MLA_Q_RANK)),
        "w_q_up": nrm(ks[7], (DEPTH, MLA_Q_RANK, MLA_HEADS * (MLA_NOPE_DIM + MLA_ROPE_DIM)), MLA_Q_RANK ** -0.5),
        "g_kv_norm": gain(ks[8], (DEPTH, MLA_KV_RANK)),
        "w_kv_up": nrm(ks[9], (DEPTH, MLA_KV_RANK, MLA_HEADS * (MLA_NOPE_DIM + MLA_V_DIM)), MLA_KV_RANK ** -0.5),
        "w_dw": nrm(ks[10], (DEPTH, CONV_WIDTH, 1, CONV_CHANNELS), CONV_WIDTH ** -0.5),
        "b_dw": nrm(ks[11], (DEPTH, CONV_CHANNELS), 0.02),
        "g_conv_ln": gain(ks[12], (DEPTH, CONV_CHANNELS)),
        "b_conv_ln": nrm(ks[13], (DEPTH, CONV_CHANNELS), 0.02),
        "w_branch": nrm(ks[14], (DEPTH, N_BRANCHES, BRANCH_WIDTH, D_MODEL), BRANCH_WIDTH ** -0.5),
        "w_out": nrm(ks[15], (DEPTH, D_MODEL, D_MODEL), D_MODEL ** -0.5),
        "g_mlp": gain(ks[16], (DEPTH, D_MODEL)),
        "w_up": nrm(ks[17], (DEPTH, D_MODEL, D_FF), D_MODEL ** -0.5),
        "w_down": nrm(ks[18], (DEPTH, D_FF, D_MODEL), D_FF ** -0.5),
    }

def first_block(x, positions, rel_bias, g_final, g_mix, w_in, swa_sinks, g_q_norm, w_q_up,
              g_kv_norm, w_kv_up, w_dw, b_dw, g_conv_ln, b_conv_ln, w_branch, w_out,
              g_mlp, w_up, w_down):
    b, s, _ = x.shape
    swa_bias, swa_mask = swa_bias_and_mask(positions, rel_bias)
    for l in range(DEPTH):
        h = rms_norm(x, g_mix[l])
        q_a, k_a, v_a, u_b, cq_c, ckv_c, kpe_c, gate_logits = jnp.split(h @ w_in[l], IN_SPLIT_POINTS, axis=-1)
        y_a = swa_attention(q_a, k_a, v_a, swa_sinks[l], swa_bias, swa_mask)
        y_b = conformer_conv(u_b, w_dw[l], b_dw[l], g_conv_ln[l], b_conv_ln[l])
        y_c = mla_attention(cq_c, ckv_c, kpe_c, positions, g_q_norm[l], w_q_up[l],
                            g_kv_norm[l], w_kv_up[l])
        branches = jnp.einsum('bsnc,ncd->bsnd', jnp.stack([y_a, y_b, y_c], axis=2), w_branch[l])
        gates = jax.nn.sigmoid(gate_logits.reshape(b, s, N_BRANCHES, D_MODEL))
        x = x + jnp.einsum('bsnd,bsnd->bsd', gates, branches) @ w_out[l]
        h = rms_norm(x, g_mlp[l])
        x = x + jnp.square(jax.nn.relu(h @ w_up[l])) @ w_down[l]
    return rms_norm(x, g_final)


GRID_W = 64
CTX_LEN = 256
F32 = jnp.float32

A_HEADS = 4
A_QK_DIM = 64
A_V_DIM = 2 * A_QK_DIM
A_WIDTH = A_HEADS * A_V_DIM
A_PROJ = 2 * (A_HEADS * 2 * A_QK_DIM) + A_WIDTH

B_HEADS = 8
B_HEAD = 64
B_WIDTH = B_HEADS * B_HEAD
B_DECAY_LORA = 64
B_AAA_LORA = 64
B_GATE_LORA = 128
B_GN_EPS = 64e-5
B_PROJ = 3 * B_WIDTH + B_DECAY_LORA + B_AAA_LORA + B_GATE_LORA

C_HEADS = 8
C_HEAD = 64
C_WIDTH = C_HEADS * C_HEAD
C_GROUPS = 2
C_REP = C_HEADS // C_GROUPS
C_STATE = 128
C_CONV = 5
C_CHUNK = 128
C_CONV_DIM = C_WIDTH + 2 * C_GROUPS * C_STATE
C_PROJ = C_WIDTH + C_CONV_DIM + 2 * C_HEADS

D_HEADS = 4
D_KEY = 64
D_VAL = 128
D_WIDTH = D_HEADS * D_VAL
D_GATE_LORA = 16
D_GATE_TAU = 16.0
D_CHUNK = 64
D_PROJ = 2 * D_HEADS * D_KEY + 2 * D_WIDTH + D_GATE_LORA

MLP_HIDDEN = 4 * D_MODEL
EVEN_IN = A_PROJ + B_PROJ
ODD_IN = C_PROJ + D_PROJ
MIX_WIDTH = A_WIDTH + B_WIDTH


def rmsnorm(x, g, eps=EPS):
    xf = x.astype(F32)
    y = xf * lax.rsqrt(jnp.mean(xf * xf, axis=-1, keepdims=True) + eps)
    return (y * g.astype(F32)).astype(x.dtype)

def _split(t, sizes):
    idx = [int(s) for s in np.cumsum(sizes)[:-1]]
    return jnp.split(t, idx, axis=-1)

def _flip_seq(*ts):
    return tuple(jnp.flip(t, axis=1) for t in ts)

def axial_rope_tables(n, dim):
    rows = n // GRID_W
    t = jnp.arange(rows * GRID_W)
    row = (t // GRID_W).astype(F32)
    col = (t % GRID_W).astype(F32)
    nf = dim // 4
    inv = ROPE_THETA ** (-jnp.arange(nf, dtype=F32) / nf)
    ar = row[:, None] * inv[None, :]
    ac = col[:, None] * inv[None, :]
    return jnp.cos(ar), jnp.sin(ar), jnp.cos(ac), jnp.sin(ac)

def _rot_half(x, cos, sin):
    x1, x2 = jnp.split(x, 2, axis=-1)
    return jnp.concatenate([x1 * cos - x2 * sin, x2 * cos + x1 * sin], axis=-1)

def apply_axial_rope(x, tabs):
    cr, sr, cc, sc = tabs
    xr, xc = jnp.split(x.astype(F32), 2, axis=-1)
    return jnp.concatenate([_rot_half(xr, cr, sr), _rot_half(xc, cc, sc)], axis=-1)

def _diff_softmax_mix(q, k, v, lam):
    s = jnp.einsum('bhmqd,bhmkd->bhmqk', q.astype(F32), k.astype(F32)) * (A_QK_DIM ** -0.5)
    p = jax.nn.softmax(s, axis=-1)
    w = p[:, :, 0] - lam * p[:, :, 1]
    return jnp.einsum('bhqk,bhkd->bhqd', w, v.astype(F32))

def diff_attention(t_lat, t_ctx, lam_q1, lam_k1, lam_q2, lam_k2, subln, layer_idx, need_ctx):
    bsz, n = t_lat.shape[0], t_lat.shape[1]
    lam_init = 0.8 - 0.6 * math.exp(-0.3 * layer_idx)
    lam = (jnp.exp(jnp.sum(lam_q1.astype(F32) * lam_k1.astype(F32)))
           - jnp.exp(jnp.sum(lam_q2.astype(F32) * lam_k2.astype(F32))) + lam_init)

    def heads(t):
        m = t.shape[1]
        q, k, v = _split(t, [A_HEADS * 2 * A_QK_DIM, A_HEADS * 2 * A_QK_DIM, A_WIDTH])
        q = q.reshape(bsz, m, A_HEADS, 2, A_QK_DIM).transpose(0, 2, 3, 1, 4)
        k = k.reshape(bsz, m, A_HEADS, 2, A_QK_DIM).transpose(0, 2, 3, 1, 4)
        v = v.reshape(bsz, m, A_HEADS, A_V_DIM).transpose(0, 2, 1, 3)
        return q, k, v

    q_l, k_l, v_l = heads(t_lat)
    q_c, k_c, v_c = heads(t_ctx)
    tabs = axial_rope_tables(n, A_QK_DIM)
    q_l = apply_axial_rope(q_l, tabs)
    k_l = apply_axial_rope(k_l, tabs)
    k_all = jnp.concatenate([k_c.astype(F32), k_l], axis=3)
    v_all = jnp.concatenate([v_c, v_l], axis=2)
    nb = n // Q_BLOCK
    qb = jnp.moveaxis(q_l.reshape(bsz, A_HEADS, 2, nb, Q_BLOCK, A_QK_DIM), 3, 0)
    ob = lax.map(lambda qq: _diff_softmax_mix(qq, k_all, v_all, lam), qb)
    o_l = jnp.moveaxis(ob, 0, 2).reshape(bsz, A_HEADS, n, A_V_DIM)

    def post(o):
        o = rmsnorm(o, subln, eps=1e-5) * (1.0 - lam_init)
        return o.transpose(0, 2, 1, 3).reshape(bsz, o.shape[2], A_WIDTH)

    out_l = post(o_l)
    out_c = post(_diff_softmax_mix(q_c, k_c, v_c, lam)) if need_ctx else None
    return out_l, out_c

def _token_shift_mix(f, mu):
    prev = jnp.pad(f[:, :-1], ((0, 0), (1, 0), (0, 0)))
    nxt = jnp.pad(f[:, 1:], ((0, 0), (0, 1), (0, 0)))
    return f + (0.5 * (prev + nxt) - f) * mu

def _rwkv7_scan(S0, r, w, k, v, kk, a):
    def step(S, inp):
        r_t, w_t, k_t, v_t, kk_t, a_t = inp
        sa = jnp.einsum('bhvk,bhk->bhv', S, kk_t)
        S = (S * w_t[:, :, None, :] - sa[..., None] * (kk_t * a_t)[:, :, None, :]
             + v_t[..., None] * k_t[:, :, None, :])
        return S, jnp.einsum('bhvk,bhk->bhv', S, r_t)
    xs = tuple(jnp.swapaxes(t, 0, 1) for t in (r, w, k, v, kk, a))
    S, ys = lax.scan(step, S0, xs)
    return jnp.swapaxes(ys, 0, 1), S

def rwkv7_mix(t_lat, t_ctx, mu, w0_f, w2_f, w0_b, w2_b, a0, a2, g2, k_k, k_a, r_k, lnx_w, lnx_b, need_ctx):
    def prep(t):
        bsz, n = t.shape[0], t.shape[1]
        f = _token_shift_mix(t, mu).astype(F32)
        r, k, v, wd, ad, gd = _split(f, [B_WIDTH, B_WIDTH, B_WIDTH, B_DECAY_LORA, B_AAA_LORA, B_GATE_LORA])
        hd = lambda u: u.reshape(bsz, n, B_HEADS, B_HEAD)
        a = jax.nn.sigmoid(a0 + ad @ a2)
        tw = jnp.tanh(wd)
        def decay(w0, w2):
            wl = -jax.nn.softplus(-(w0 + tw @ w2)) - 0.5
            return hd(jnp.exp(-jnp.exp(wl)))
        kk = hd(k * k_k)
        kk = kk / jnp.maximum(jnp.sqrt(jnp.sum(kk * kk, axis=-1, keepdims=True)), 1e-12)
        k = k * (1.0 + (a - 1.0) * k_a)
        g = jax.nn.sigmoid(gd) @ g2
        return (hd(r), hd(k), hd(v), kk, hd(a), decay(w0_f, w2_f), decay(w0_b, w2_b), g)

    r_c, k_c, v_c, kk_c, a_c, wf_c, wb_c, g_c = prep(t_ctx)
    r_l, k_l, v_l, kk_l, a_l, wf_l, wb_l, g_l = prep(t_lat)
    S0 = jnp.zeros((t_lat.shape[0], B_HEADS, B_HEAD, B_HEAD), F32)
    yf_c, Sf_c = _rwkv7_scan(S0, r_c, wf_c, k_c, v_c, kk_c, a_c)
    yb_c, Sb_c = _rwkv7_scan(S0, *_flip_seq(r_c, wb_c, k_c, v_c, kk_c, a_c))
    yf_l, _ = _rwkv7_scan(Sf_c, r_l, wf_l, k_l, v_l, kk_l, a_l)
    yb_l, _ = _rwkv7_scan(Sb_c, *_flip_seq(r_l, wb_l, k_l, v_l, kk_l, a_l))

    def post(r, k, v, g, yf, yb):
        bsz, n = r.shape[0], r.shape[1]
        y = yf + jnp.flip(yb, axis=1)
        mean = jnp.mean(y, axis=-1, keepdims=True)
        var = jnp.mean(jnp.square(y - mean), axis=-1, keepdims=True)
        y = ((y - mean) * lax.rsqrt(var + B_GN_EPS)).reshape(bsz, n, B_WIDTH) * lnx_w + lnx_b
        bonus = jnp.sum(r * k * r_k.reshape(B_HEADS, B_HEAD), axis=-1, keepdims=True) * v
        return (y + bonus.reshape(bsz, n, B_WIDTH)) * g

    out_l = post(r_l, k_l, v_l, g_l, yf_l, yb_l)
    out_c = post(r_c, k_c, v_c, g_c, yf_c, yb_c) if need_ctx else None
    return out_l, out_c

def _dwconv_centred(t, w, b):
    y = lax.conv_general_dilated(t, w[:, None, :].astype(t.dtype), window_strides=(1,),
                                 padding=[(C_CONV // 2, C_CONV // 2)],
                                 dimension_numbers=('NWC', 'WIO', 'NWC'),
                                 feature_group_count=t.shape[-1])
    return y + b

def _ssd_chunk_scan(h0, x, dt, la, bm, cm):
    bsz, n = x.shape[0], x.shape[1]
    nc = n // C_CHUNK
    chunks = lambda t: jnp.swapaxes(t.reshape((bsz, nc, C_CHUNK) + t.shape[2:]), 0, 1)
    idx = jnp.arange(C_CHUNK)
    lower = (idx[:, None] >= idx[None, :])[None, :, :, None, None]

    def step(h, inp):
        xc, dtc, lac, bc, cc = inp
        cum = jnp.cumsum(lac, axis=1)
        lmat = jnp.exp(jnp.where(lower, cum[:, :, None] - cum[:, None, :], -jnp.inf))
        cb = jnp.einsum('bign,bjgn->bijg', cc, bc)
        xdt = xc * dtc[..., None]
        y = jnp.einsum('bijgr,bjgrp->bigrp', cb[..., None] * lmat, xdt)
        y = y + jnp.einsum('bign,bgrpn->bigrp', cc, h) * jnp.exp(cum)[..., None]
        w_end = jnp.exp(cum[:, -1:] - cum)
        h = h * jnp.exp(cum[:, -1])[..., None, None] + jnp.einsum('bjgn,bjgrp->bgrpn', bc, xdt * w_end[..., None])
        return h, y

    h, ys = lax.scan(step, h0, tuple(chunks(t) for t in (x, dt, la, bm, cm)))
    return jnp.swapaxes(ys, 0, 1).reshape(x.shape), h

def ssd_mix(t_lat, t_ctx, conv_w, conv_b, dt_bias_f, a_log_f, dt_bias_b, a_log_b, d_skip, norm_g, need_ctx):
    def prep(t):
        bsz, n = t.shape[0], t.shape[1]
        z, xbc, dt_f, dt_b = _split(t, [C_WIDTH, C_CONV_DIM, C_HEADS, C_HEADS])
        xbc = jax.nn.silu(_dwconv_centred(xbc, conv_w, conv_b).astype(F32))
        xs, bm, cm = _split(xbc, [C_WIDTH, C_GROUPS * C_STATE, C_GROUPS * C_STATE])
        xs = xs.reshape(bsz, n, C_GROUPS, C_REP, C_HEAD)
        bm = bm.reshape(bsz, n, C_GROUPS, C_STATE)
        cm = cm.reshape(bsz, n, C_GROUPS, C_STATE)
        def direction(dt_raw, dt_bias, a_log):
            dt = jax.nn.softplus(dt_raw.astype(F32) + dt_bias).reshape(bsz, n, C_GROUPS, C_REP)
            return dt, dt * (-jnp.exp(a_log.astype(F32))).reshape(C_GROUPS, C_REP)
        return z, xs, bm, cm, direction(dt_f, dt_bias_f, a_log_f), direction(dt_b, dt_bias_b, a_log_b)

    z_c, x_c, b_c, c_c, (dtf_c, laf_c), (dtb_c, lab_c) = prep(t_ctx)
    z_l, x_l, b_l, c_l, (dtf_l, laf_l), (dtb_l, lab_l) = prep(t_lat)
    h0 = jnp.zeros((t_lat.shape[0], C_GROUPS, C_REP, C_HEAD, C_STATE), F32)
    yf_c, hf_c = _ssd_chunk_scan(h0, x_c, dtf_c, laf_c, b_c, c_c)
    yb_c, hb_c = _ssd_chunk_scan(h0, *_flip_seq(x_c, dtb_c, lab_c, b_c, c_c))
    yf_l, _ = _ssd_chunk_scan(hf_c, x_l, dtf_l, laf_l, b_l, c_l)
    yb_l, _ = _ssd_chunk_scan(hb_c, *_flip_seq(x_l, dtb_l, lab_l, b_l, c_l))

    def post(z, xs, yf, yb):
        bsz, n = xs.shape[0], xs.shape[1]
        y = yf + jnp.flip(yb, axis=1) + xs * d_skip.astype(F32).reshape(C_GROUPS, C_REP, 1)
        y = y.reshape(bsz, n, C_WIDTH) * jax.nn.silu(z.astype(F32))
        y = rmsnorm(y.reshape(bsz, n, C_GROUPS, C_WIDTH // C_GROUPS), norm_g.reshape(C_GROUPS, C_WIDTH // C_GROUPS))
        return y.reshape(bsz, n, C_WIDTH)

    out_l = post(z_l, x_l, yf_l, yb_l)
    out_c = post(z_c, x_c, yf_c, yb_c) if need_ctx else None
    return out_l, out_c

def _gla_chunk_scan(S0, q, k, v, lg):
    bsz, n = q.shape[0], q.shape[1]
    nc = n // D_CHUNK
    chunks = lambda t: jnp.swapaxes(t.reshape((bsz, nc, D_CHUNK) + t.shape[2:]), 0, 1)
    idx = jnp.arange(D_CHUNK)
    lower = (idx[:, None] >= idx[None, :])[None, :, :, None, None]

    def step(S, inp):
        qc, kc, vc, gc = inp
        cum = jnp.cumsum(gc, axis=1)
        dec = jnp.exp(jnp.where(lower, cum[:, :, None] - cum[:, None, :], -jnp.inf))
        att = jnp.einsum('bihk,bjhk,bijhk->bhij', qc, kc, dec)
        y = jnp.einsum('bhij,bjhv->bihv', att, vc) + jnp.einsum('bihk,bhkv->bihv', qc * jnp.exp(cum), S)
        S = S * jnp.exp(cum[:, -1])[..., None] + jnp.einsum('bjhk,bjhv->bhkv', kc * jnp.exp(cum[:, -1:] - cum), vc)
        return S, y

    S, ys = lax.scan(step, S0, tuple(chunks(t) for t in (q, k, v, lg)))
    return jnp.swapaxes(ys, 0, 1).reshape(v.shape), S

def gla_mix(t_lat, t_ctx, gk_up_f, gk_b_f, gk_up_b, gk_b_b, norm_g, need_ctx):
    def prep(t):
        bsz, n = t.shape[0], t.shape[1]
        q, k, v, g, gd = _split(t.astype(F32), [D_HEADS * D_KEY, D_HEADS * D_KEY, D_WIDTH, D_WIDTH, D_GATE_LORA])
        hk = lambda u: u.reshape(bsz, n, D_HEADS, D_KEY)
        def log_gate(up, b):
            return hk(jax.nn.log_sigmoid(gd @ up + b) / D_GATE_TAU)
        return (hk(q) * (D_KEY ** -0.5), hk(k), v.reshape(bsz, n, D_HEADS, D_VAL), g,
                log_gate(gk_up_f, gk_b_f), log_gate(gk_up_b, gk_b_b))

    q_c, k_c, v_c, g_c, gf_c, gb_c = prep(t_ctx)
    q_l, k_l, v_l, g_l, gf_l, gb_l = prep(t_lat)
    S0 = jnp.zeros((t_lat.shape[0], D_HEADS, D_KEY, D_VAL), F32)
    yf_c, Sf_c = _gla_chunk_scan(S0, q_c, k_c, v_c, gf_c)
    yb_c, Sb_c = _gla_chunk_scan(S0, *_flip_seq(q_c, k_c, v_c, gb_c))
    yf_l, _ = _gla_chunk_scan(Sf_c, q_l, k_l, v_l, gf_l)
    yb_l, _ = _gla_chunk_scan(Sb_c, *_flip_seq(q_l, k_l, v_l, gb_l))

    def post(g, yf, yb):
        bsz, n = g.shape[0], g.shape[1]
        y = rmsnorm(yf + jnp.flip(yb, axis=1), norm_g)
        return y.reshape(bsz, n, D_WIDTH) * jax.nn.silu(g)

    out_l = post(g_l, yf_l, yb_l)
    out_c = post(g_c, yf_c, yb_c) if need_ctx else None
    return out_l, out_c

def even_mixer(p_lat, p_ctx, lam_q1, lam_k1, lam_q2, lam_k2, subln, mu, w0_f, w2_f, w0_b, w2_b,
               a0, a2, g2, k_k, k_a, r_k, lnx_w, lnx_b, layer_idx, need_ctx):
    oa_l, oa_c = diff_attention(p_lat[..., :A_PROJ], p_ctx[..., :A_PROJ],
                                lam_q1, lam_k1, lam_q2, lam_k2, subln, layer_idx, need_ctx)
    ob_l, ob_c = rwkv7_mix(p_lat[..., A_PROJ:], p_ctx[..., A_PROJ:], mu, w0_f, w2_f, w0_b, w2_b,
                           a0, a2, g2, k_k, k_a, r_k, lnx_w, lnx_b, need_ctx)
    o_l = jnp.concatenate([oa_l, ob_l], axis=-1)
    o_c = jnp.concatenate([oa_c, ob_c], axis=-1) if need_ctx else None
    return o_l, o_c

def odd_mixer(p_lat, p_ctx, conv_w, conv_b, dt_bias_f, a_log_f, dt_bias_b, a_log_b, d_skip, ssm_norm,
              gk_up_f, gk_b_f, gk_up_b, gk_b_b, gla_norm, need_ctx):
    oc_l, oc_c = ssd_mix(p_lat[..., :C_PROJ], p_ctx[..., :C_PROJ], conv_w, conv_b, dt_bias_f, a_log_f,
                         dt_bias_b, a_log_b, d_skip, ssm_norm, need_ctx)
    od_l, od_c = gla_mix(p_lat[..., C_PROJ:], p_ctx[..., C_PROJ:], gk_up_f, gk_b_f, gk_up_b, gk_b_b,
                         gla_norm, need_ctx)
    o_l = jnp.concatenate([oc_l, od_l], axis=-1)
    o_c = jnp.concatenate([oc_c, od_c], axis=-1) if need_ctx else None
    return o_l, o_c

def _ada(x, g, shift, scale):
    return rmsnorm(x, g) * (1.0 + scale) + shift

def _sq_relu_mlp(h, w1, w2):
    return jnp.square(jax.nn.relu(h @ w1)) @ w2

def second_inputs(seed: int = 0) -> dict:
    key = jax.random.key(seed)
    keys = iter(jax.random.split(key, 64))
    D = D_MODEL
    def nrm(shape, scale):
        return jax.random.normal(next(keys), shape, F32) * scale
    def gain(n):
        return 1.0 + 0.05 * jax.random.normal(next(keys), (n,), F32)
    def unif(shape, lo, hi):
        return jax.random.uniform(next(keys), shape, F32, lo, hi)
    def dt_bias(n):
        dt = jnp.exp(unif((n,), math.log(1e-3), math.log(1e-1)))
        return dt + jnp.log(-jnp.expm1(-dt))
    inp = {}
    inp['x'] = nrm((BATCH, SEQ, D), 1.0)
    inp['c'] = nrm((BATCH, D), 1.0)
    inp['ctx'] = nrm((BATCH, CTX_LEN, D), 1.0)
    inp['c_ctx'] = nrm((D,), 1.0)
    inp['l0_mod_w'] = nrm((D, 6 * D), 0.5 * D ** -0.5)
    inp['l0_mod_b'] = nrm((6 * D,), 0.02)
    inp['l0_norm1'] = gain(D)
    inp['l0_norm2'] = gain(D)
    inp['l0_w_in'] = nrm((D, EVEN_IN), D ** -0.5)
    inp['l0_w_out'] = nrm((MIX_WIDTH, D), MIX_WIDTH ** -0.5)
    inp['l0_mlp_w1'] = nrm((D, MLP_HIDDEN), D ** -0.5)
    inp['l0_mlp_w2'] = nrm((MLP_HIDDEN, D), MLP_HIDDEN ** -0.5)
    inp['l0_lam_q1'] = nrm((A_QK_DIM,), 0.1)
    inp['l0_lam_k1'] = nrm((A_QK_DIM,), 0.1)
    inp['l0_lam_q2'] = nrm((A_QK_DIM,), 0.1)
    inp['l0_lam_k2'] = nrm((A_QK_DIM,), 0.1)
    inp['l0_subln'] = gain(A_V_DIM)
    inp['l0_mu'] = unif((B_PROJ,), 0.0, 1.0)
    inp['l0_w0_f'] = unif((B_WIDTH,), -6.0, -1.0)
    inp['l0_w2_f'] = nrm((B_DECAY_LORA, B_WIDTH), 0.1 * B_DECAY_LORA ** -0.5)
    inp['l0_w0_b'] = unif((B_WIDTH,), -6.0, -1.0)
    inp['l0_w2_b'] = nrm((B_DECAY_LORA, B_WIDTH), 0.1 * B_DECAY_LORA ** -0.5)
    inp['l0_a0'] = nrm((B_WIDTH,), 0.1)
    inp['l0_a2'] = nrm((B_AAA_LORA, B_WIDTH), B_AAA_LORA ** -0.5)
    inp['l0_g2'] = nrm((B_GATE_LORA, B_WIDTH), B_GATE_LORA ** -0.5)
    inp['l0_k_k'] = 0.85 + nrm((B_WIDTH,), 0.05)
    inp['l0_k_a'] = gain(B_WIDTH)
    inp['l0_r_k'] = nrm((B_WIDTH,), 0.1)
    inp['l0_lnx_w'] = gain(B_WIDTH)
    inp['l0_lnx_b'] = nrm((B_WIDTH,), 0.02)
    inp['l1_mod_w'] = nrm((D, 6 * D), 0.5 * D ** -0.5)
    inp['l1_mod_b'] = nrm((6 * D,), 0.02)
    inp['l1_norm1'] = gain(D)
    inp['l1_norm2'] = gain(D)
    inp['l1_w_in'] = nrm((D, ODD_IN), D ** -0.5)
    inp['l1_w_out'] = nrm((MIX_WIDTH, D), MIX_WIDTH ** -0.5)
    inp['l1_mlp_w1'] = nrm((D, MLP_HIDDEN), D ** -0.5)
    inp['l1_mlp_w2'] = nrm((MLP_HIDDEN, D), MLP_HIDDEN ** -0.5)
    inp['l1_conv_w'] = nrm((C_CONV, C_CONV_DIM), C_CONV ** -0.5)
    inp['l1_conv_b'] = nrm((C_CONV_DIM,), 0.02)
    inp['l1_dt_bias_f'] = dt_bias(C_HEADS)
    inp['l1_a_log_f'] = jnp.log(unif((C_HEADS,), 1.0, 16.0))
    inp['l1_dt_bias_b'] = dt_bias(C_HEADS)
    inp['l1_a_log_b'] = jnp.log(unif((C_HEADS,), 1.0, 16.0))
    inp['l1_d_skip'] = gain(C_HEADS)
    inp['l1_ssm_norm'] = gain(C_WIDTH)
    inp['l1_gk_up_f'] = nrm((D_GATE_LORA, D_HEADS * D_KEY), D_GATE_LORA ** -0.5)
    inp['l1_gk_b_f'] = nrm((D_HEADS * D_KEY,), 0.1)
    inp['l1_gk_up_b'] = nrm((D_GATE_LORA, D_HEADS * D_KEY), D_GATE_LORA ** -0.5)
    inp['l1_gk_b_b'] = nrm((D_HEADS * D_KEY,), 0.1)
    inp['l1_gla_norm'] = gain(D_VAL)
    inp['final_norm'] = gain(D)
    return inp

def second_block(x, c, ctx, c_ctx,
              l0_mod_w, l0_mod_b, l0_norm1, l0_norm2, l0_w_in, l0_w_out, l0_mlp_w1, l0_mlp_w2,
              l0_lam_q1, l0_lam_k1, l0_lam_q2, l0_lam_k2, l0_subln,
              l0_mu, l0_w0_f, l0_w2_f, l0_w0_b, l0_w2_b, l0_a0, l0_a2, l0_g2, l0_k_k, l0_k_a, l0_r_k,
              l0_lnx_w, l0_lnx_b,
              l1_mod_w, l1_mod_b, l1_norm1, l1_norm2, l1_w_in, l1_w_out, l1_mlp_w1, l1_mlp_w2,
              l1_conv_w, l1_conv_b, l1_dt_bias_f, l1_a_log_f, l1_dt_bias_b, l1_a_log_b, l1_d_skip, l1_ssm_norm,
              l1_gk_up_f, l1_gk_b_f, l1_gk_up_b, l1_gk_b_b, l1_gla_norm,
              final_norm):
    shared = [
        (l0_mod_w, l0_mod_b, l0_norm1, l0_norm2, l0_w_in, l0_w_out, l0_mlp_w1, l0_mlp_w2),
        (l1_mod_w, l1_mod_b, l1_norm1, l1_norm2, l1_w_in, l1_w_out, l1_mlp_w1, l1_mlp_w2),
    ]
    for i in range(DEPTH):
        mod_w, mod_b, norm1, norm2, w_in, w_out, mlp_w1, mlp_w2 = shared[i]
        need_ctx = i < DEPTH - 1
        m_l = (jax.nn.silu(c) @ mod_w + mod_b)[:, None, :]
        m_c = jax.nn.silu(c_ctx) @ mod_w + mod_b
        sh1_l, sc1_l, g1_l, sh2_l, sc2_l, g2_l = jnp.split(m_l, 6, axis=-1)
        sh1_c, sc1_c, g1_c, sh2_c, sc2_c, g2_c = jnp.split(m_c, 6, axis=-1)
        p_lat = _ada(x, norm1, sh1_l, sc1_l) @ w_in
        p_ctx = _ada(ctx, norm1, sh1_c, sc1_c) @ w_in
        if i % 2 == 0:
            o_l, o_c = even_mixer(p_lat, p_ctx, l0_lam_q1, l0_lam_k1, l0_lam_q2, l0_lam_k2, l0_subln,
                                  l0_mu, l0_w0_f, l0_w2_f, l0_w0_b, l0_w2_b, l0_a0, l0_a2, l0_g2,
                                  l0_k_k, l0_k_a, l0_r_k, l0_lnx_w, l0_lnx_b, i, need_ctx)
        else:
            o_l, o_c = odd_mixer(p_lat, p_ctx, l1_conv_w, l1_conv_b, l1_dt_bias_f, l1_a_log_f,
                                 l1_dt_bias_b, l1_a_log_b, l1_d_skip, l1_ssm_norm,
                                 l1_gk_up_f, l1_gk_b_f, l1_gk_up_b, l1_gk_b_b, l1_gla_norm, need_ctx)
        x = x + g1_l * (o_l.astype(x.dtype) @ w_out)
        x = x + g2_l * _sq_relu_mlp(_ada(x, norm2, sh2_l, sc2_l), mlp_w1, mlp_w2)
        if need_ctx:
            ctx = ctx + g1_c * (o_c.astype(ctx.dtype) @ w_out)
            ctx = ctx + g2_c * _sq_relu_mlp(_ada(ctx, norm2, sh2_c, sc2_c), mlp_w1, mlp_w2)
    return rmsnorm(x, final_norm)


def setup_inputs(seed=0):
    out = dict(first_inputs(seed))
    for name, value in second_inputs(seed + 1).items():
        if name != "x":
            out[name + "_2"] = value
    return out


def reference(
    x, positions, rel_bias, g_final, g_mix, w_in, swa_sinks, g_q_norm, w_q_up, g_kv_norm,
    w_kv_up, w_dw, b_dw, g_conv_ln, b_conv_ln, w_branch, w_out, g_mlp, w_up, w_down, c_2, ctx_2,
    c_ctx_2, l0_mod_w_2, l0_mod_b_2, l0_norm1_2, l0_norm2_2, l0_w_in_2, l0_w_out_2, l0_mlp_w1_2,
    l0_mlp_w2_2, l0_lam_q1_2, l0_lam_k1_2, l0_lam_q2_2, l0_lam_k2_2, l0_subln_2, l0_mu_2,
    l0_w0_f_2, l0_w2_f_2, l0_w0_b_2, l0_w2_b_2, l0_a0_2, l0_a2_2, l0_g2_2, l0_k_k_2, l0_k_a_2,
    l0_r_k_2, l0_lnx_w_2, l0_lnx_b_2, l1_mod_w_2, l1_mod_b_2, l1_norm1_2, l1_norm2_2, l1_w_in_2,
    l1_w_out_2, l1_mlp_w1_2, l1_mlp_w2_2, l1_conv_w_2, l1_conv_b_2, l1_dt_bias_f_2,
    l1_a_log_f_2, l1_dt_bias_b_2, l1_a_log_b_2, l1_d_skip_2, l1_ssm_norm_2, l1_gk_up_f_2,
    l1_gk_b_f_2, l1_gk_up_b_2, l1_gk_b_b_2, l1_gla_norm_2, final_norm_2,
):
    x = first_block(
        x, positions, rel_bias, g_final, g_mix, w_in, swa_sinks, g_q_norm, w_q_up, g_kv_norm,
        w_kv_up, w_dw, b_dw, g_conv_ln, b_conv_ln, w_branch, w_out, g_mlp, w_up, w_down,
    )
    return second_block(
        x, c_2, ctx_2, c_ctx_2, l0_mod_w_2, l0_mod_b_2, l0_norm1_2, l0_norm2_2, l0_w_in_2,
        l0_w_out_2, l0_mlp_w1_2, l0_mlp_w2_2, l0_lam_q1_2, l0_lam_k1_2, l0_lam_q2_2,
        l0_lam_k2_2, l0_subln_2, l0_mu_2, l0_w0_f_2, l0_w2_f_2, l0_w0_b_2, l0_w2_b_2, l0_a0_2,
        l0_a2_2, l0_g2_2, l0_k_k_2, l0_k_a_2, l0_r_k_2, l0_lnx_w_2, l0_lnx_b_2, l1_mod_w_2,
        l1_mod_b_2, l1_norm1_2, l1_norm2_2, l1_w_in_2, l1_w_out_2, l1_mlp_w1_2, l1_mlp_w2_2,
        l1_conv_w_2, l1_conv_b_2, l1_dt_bias_f_2, l1_a_log_f_2, l1_dt_bias_b_2, l1_a_log_b_2,
        l1_d_skip_2, l1_ssm_norm_2, l1_gk_up_f_2, l1_gk_b_f_2, l1_gk_up_b_2, l1_gk_b_b_2,
        l1_gla_norm_2, final_norm_2,
    )


_drawn_inputs = setup_inputs


def setup_inputs(seed=0):
    import zlib

    import numpy as np

    out = dict(_drawn_inputs(seed))
    spreads = {}
    factors = {'swa_sinks': 8.0,
     'g_q_norm': 8.0,
     'g_kv_norm': 5.289,
     'b_dw': 2.92,
     'b_conv_ln': 5.789,
     'l0_norm1_2': 4.492,
     'l0_lam_q1_2': 5.845,
     'l0_lam_k1_2': 3.059,
     'l0_lam_q2_2': 8.0,
     'l0_lam_k2_2': 8.0,
     'l0_subln_2': 5.529,
     'l0_w2_f_2': 8.0,
     'l0_w2_b_2': 8.0,
     'l0_a0_2': 8.0,
     'l0_lnx_w_2': 8.0,
     'l0_lnx_b_2': 30.43,
     'l1_norm1_2': 2.926,
     'l1_norm2_2': 3.063,
     'l1_conv_b_2': 28.349,
     'l1_a_log_f_2': 3.648,
     'l1_d_skip_2': 64.0,
     'l1_ssm_norm_2': 25.604,
     'l1_gk_b_f_2': 8.0,
     'l1_gk_b_b_2': 8.0,
     'l1_gla_norm_2': 8.0,
     'l0_norm2_2': 4.138}
    for name, (base, spread) in spreads.items():
        noise = np.random.default_rng([zlib.crc32(name.encode()), seed]).standard_normal(out[name].shape)
        drawn = base * np.exp(spread * noise) if base else spread * noise
        out[name] = __import__('jax').numpy.asarray(drawn.astype(out[name].dtype))
    for name, factor in factors.items():
        out[name] = (out[name] * factor).astype(out[name].dtype)
    return out
```

```python
import math
from contextlib import ExitStack

import numpy as np

import concourse.bass as bass
from concourse import mybir

F32 = mybir.dt.float32
F32R = mybir.dt.float32r
I32 = mybir.dt.int32
ALU = mybir.AluOpType
ACT = mybir.ActivationFunctionType
AX = mybir.AxisListType.X

P = 128
BANK = 512
D_MODEL, SEQ, CTX, DEPTH, D_FF = 1024, 512, 256, 2, 4096
KD = D_MODEL // P
EPS = 1e-6
MASKED = -1e30
RING_FLOATS = 9216


def _const_table():
    parts, at, col = [], {}, 0

    def put(name, a):
        nonlocal col
        a = np.asarray(a, np.float32)
        full = np.zeros((P, a.shape[1]), np.float32)
        full[:a.shape[0]] = a
        parts.append(full)
        at[name] = (col, a.shape[1])
        col += a.shape[1]

    i = np.arange(P)
    put("ident", np.eye(P))
    put("ones", np.ones((P, P)))
    put("head_ones", (i[:, None] // 64 == i[None, :] // 64))
    put("stack", (i[:, None] % 64 == np.arange(64)[None, :]))
    put("causal", np.where(i[None, :] <= i[:, None], 0.0, MASKED))
    put("no_prev", np.where(i[None, :] >= 127 - i[:, None], 0.0, MASKED))
    r = np.zeros((P, 32))
    for d in range(16):
        r[64 + d + 16, d] = -1.0
        r[64 + d, d + 16] = 1.0
    put("mla_rot", r)
    half = np.float32(16)
    freq = np.exp(np.float32(-math.log(10000.0)) * np.arange(16, dtype=np.float32) / half)
    f = np.zeros((P, 1))
    f[64:96, 0] = np.concatenate([freq, freq])
    put("mla_freq", f)
    same = i[:, None] // 64 == i[None, :] // 64
    put("s_lt_t", same & (i[:, None] < i[None, :]))
    put("s_le_t", same & (i[:, None] <= i[None, :]))
    put("s_gt_t", same & (i[:, None] > i[None, :]))
    put("s_ge_t", same & (i[:, None] >= i[None, :]))
    for l in range(6):
        b = 1 << l
        put(f"merge{l}", (i[:, None] // (2 * b) == i[None, :] // (2 * b)) & (i[:, None] // b > i[None, :] // b))
        put(f"mergeT{l}", (i[:, None] // (2 * b) == i[None, :] // (2 * b)) & (i[:, None] // b < i[None, :] // b))
    put("j_le_i", i[:, None] <= i[None, :])
    put("j_ge_i", i[:, None] >= i[None, :])
    return np.concatenate(parts, 1), at


def _axial_table():
    r = np.zeros((P, P), np.float32)
    for d in range(P):
        if d % 32 < 16:
            r[d + 16, d] = -1.0
        else:
            r[d - 16, d] = 1.0
    
    inv = np.float32(10000.0) ** (-np.arange(16, dtype=np.float32) / np.float32(16))
    tok = np.arange(SEQ)
    row, colm = (tok // 64).astype(np.float32), (tok % 64).astype(np.float32)
    ang = np.zeros((P, SEQ), np.float32)
    for d in range(P):
        ang[d] = (row if d % 64 < 32 else colm) * inv[d % 16]
    return np.concatenate([r, np.cos(ang), np.sin(ang)], 1)


CONSTS, CONST_AT = _const_table()
AXIAL = _axial_table()


class Phases:

    def __init__(self, nc):
        self.nc, self.n, self.stale, self.live = nc, 0, [], []
        self.cleared = None

    def sem(self, name):
        cm = self.nc.semaphore(f"{name}_{self.n}")
        self.n += 1
        self.live.append((cm, cm.__enter__()))
        return self.live[-1][1]

    def held_sem(self, name):
        handle = self.sem(name)
        return handle, self.live.pop()

    def __enter__(self):
        self.closing, self.stale = self.stale, []
        self.cm = self.nc.Block()
        self.block = self.cm.__enter__()
        closing = self.closing

        @self.block.gpsimd
        def _(pool):
            for _, handle in closing:
                pool.sem_clear(handle)

        return self.block

    def __exit__(self, *a):
        self.cm.__exit__(*a)
        for cm, _ in self.closing:
            cm.__exit__(None, None, None)
        self.stale, self.live = self.live, []


class Chain:

    def __init__(self, eng, done):
        self.eng, self.done, self.n = eng, done, 0

    def __call__(self, ins):
        self.n += 1
        ins.then_inc(self.done, 1)
        self.eng.wait_ge(self.done, self.n)


class Kit:

    def __init__(self, nc, ctx):
        self.nc, self.ph = nc, Phases(nc)
        self.ps = ctx.enter_context(nc.psum_tensor("banks", [P, 8, BANK], F32))
        part = [2, KD, P]
        self.ring_at = -(-nc.sbuf_base // 32) * 32
        self.ring, (self.w_hi, self.w_lo) = self.shared(
            ctx, "weight_ring", [P, RING_FLOATS], [("weights_hi", part), ("weights_lo", part)])
        self.consts = ctx.enter_context(nc.sbuf_tensor("consts", [P, CONSTS.shape[1]], F32))

    def shared(self, ctx, name, shape, parts):
        at = -(-self.nc.sbuf_base // 32) * 32
        whole = ctx.enter_context(self.nc.sbuf_tensor(name, shape, F32))
        views = []
        for part, dims in parts:
            views.append(self.nc.alloc_sbuf_tensor_at(part, [P] + dims, F32R, offset=at))
            at += math.prod(dims) * 4
        return whole, views

    def const(self, name, rows=slice(0, P)):
        at, width = CONST_AT[name]
        return self.consts[rows, at:at + width]


def spans_of(tokens):
    return [(0, SEQ)] if tokens == SEQ else [(0, CTX), (CTX, SEQ)]


class Split:

    def __init__(self, kit, name, tokens, in_place=None, low_place=None):
        self.kit, self.name, self.tokens, self.in_place, self.x_lo = kit, name, tokens, in_place, low_place
        self.ctx = ExitStack()

    def __enter__(self):
        kit, nc, name, sem = self.kit, self.kit.nc, self.name, self.kit.ph.sem
        part = 2 * KD * P
        self.w_hi, self.w_lo = kit.w_hi, kit.w_lo
        self.raw = kit.ring[:, 2 * part:4 * part].rearrange("p (s k n) -> p s k n", s=2, k=KD)
        self.x_hi = self.in_place
        if self.in_place is None:
            self.x_hi = self.ctx.enter_context(nc.sbuf_tensor(f"{name}_x_hi", [P, KD, self.tokens], F32R))
        if self.x_lo is None:
            self.x_lo = self.ctx.enter_context(nc.sbuf_tensor(f"{name}_x_lo", [P, KD, self.tokens], F32R))
        self.landed = [sem(f"{name}_landed{s}") for s in range(2)]
        self.w_rounded, self.w_ready = sem(f"{name}_w_rounded"), sem(f"{name}_w_ready")
        self.x_rounded, self.x_cut, self.x_ready = (sem(f"{name}_x_{s}") for s in ("rounded", "cut", "ready"))
        return self

    def __exit__(self, *a):
        self.ctx.close()

    def _raw(self, t):
        half = slice(t % 2 * P, t % 2 * P + P)
        return self.raw[:, t // 2 % 2, :, half]

    def load(self, sp, pair, source):
        sp.dma_start(self.raw[:, pair % 2], source).then_inc(self.landed[pair % 2], 16)

    def round_weights(self, act, i, t, per_turn=4):
        pairs = per_turn // 4
        act.wait_ge(self.landed[t // 2 % 2], i * (16 * pairs) + (t // 4 + 1) * 16)
        act.activation(self.w_hi[:, t % 2], self._raw(t), ACT.Copy).then_inc(self.w_rounded, 1)

    def rest_of_weights(self, dve, i, t, per_turn=4):
        dve.wait_ge(self.w_rounded, i * per_turn + (t + 1))
        dve.tensor_tensor(self.w_lo[:, t % 2], self._raw(t), self.w_hi[:, t % 2].bitcast(F32), ALU.subtract)\
            .then_inc(self.w_ready, 1)

    def round_x(self, act, x):
        if self.in_place is None:
            for k in range(KD):
                act.activation(self.x_hi[:, k, :], x[:, k, :], ACT.Copy).then_inc(self.x_rounded, 1)
            return
        for k in range(KD + 1):
            if k < KD:
                act.activation(self.x_lo[:, k, :], x[:, k, :], ACT.Copy).then_inc(self.x_rounded, 1)
            if k > 0:
                act.wait_ge(self.x_cut, k)
                act.activation(self.x_hi[:, k - 1, :], x[:, k - 1, :], ACT.Copy).then_inc(self.x_ready, 1)

    def rest_of_x(self, dve, x):
        hi, done = (self.x_hi, self.x_ready) if self.in_place is None else (self.x_lo, self.x_cut)
        for k in range(KD):
            dve.wait_ge(self.x_rounded, k + 1)
            dve.tensor_tensor(self.x_lo[:, k, :], x[:, k, :], hi[:, k, :].bitcast(F32), ALU.subtract)\
                .then_inc(done, 1)

    def multiply(self, pe, i, t, x, banks, spans, per_turn=4, arriving=None):
        pe.wait_ge(self.w_ready, i * per_turn + (t + 1))
        x_hi, x_lo = x
        hi, lo = self.w_hi[:, t % 2], self.w_lo[:, t % 2]
        for k in range(KD):
            if arriving:
                arriving(k)
            for (t0, w), bank in zip(spans, banks):
                for n, (a, b) in enumerate(((hi, x_hi), (hi, x_lo), (lo, x_hi))):
                    mm = pe.matmul(bank, a[:, k, :], b[:, k, t0:t0 + w],
                                   start=(k == 0 and n == 0), stop=(k == KD - 1 and n == 2))
        return mm


def gemm(kit, name, weights, n_cols, rhs, tokens, evacuate, engine="scalar", **places):
    ph, ps = kit.ph, kit.ps
    n = n_cols // P
    turns = (n - 2) // 4
    rest = n - 4 * turns
    spans = spans_of(tokens)
    room = 4

    def banks(t):
        b = t % room * len(spans)
        return [ps[:, b + s, 0:w] for s, (_, w) in enumerate(spans)]

    with Split(kit, name, tokens, **places) as split:
        summed = ph.sem(f"{name}_summed")
        emptied = ph.sem(f"{name}_emptied")
        with ph as block:
            @block.sync
            def _(sp):
                split.load(sp, 0, weights[:, :, 0:256])
                split.load(sp, 1, weights[:, :, 256:512])

                def turn(i, pairs):
                    for s in range(pairs):
                        sp.wait_ge(split.w_ready, i * 4 + (2 * s - 2))
                        split.load(sp, s, weights[:, :, bass.ds(i * 512 + s * 256, 256)])

                full = n // 4
                if full > 1:
                    with sp.Fori(1, full) as i:
                        turn(i, 2)
                turn(full, n % 4 // 2)

            @block.tensor
            def _(pe):
                def turn(i, first, count=4):
                    for t in range(count):
                        if not first:
                            pe.wait_ge(emptied, i * 4 + (t + 1 - room))
                        arriving = (lambda k: pe.wait_ge(split.x_ready, k + 1)) if first and t == 0 else None
                        split.multiply(pe, i, t, (split.x_hi, split.x_lo), banks(t), spans, arriving=arriving)\
                            .then_inc(summed, 1)

                turn(0, True)
                full = n // 4
                if full > 1:
                    with pe.Fori(1, full) as i:
                        turn(i, False)
                turn(full, False, n % 4)

            def evacuation(eng, i, t):
                eng.wait_ge(summed, i * 4 + (t + 1))
                evacuate(eng, i * 4 + t, banks(t)).then_inc(emptied, 1)

            @block.scalar
            def _(act):
                split.round_weights(act, 0, 0)
                split.round_x(act, rhs)
                split.round_weights(act, 0, 1)

                def turn(i, count, more):
                    for t in range(count):
                        if t < more:
                            act.wait_ge(summed, i * 4 + (t + 1))
                            split.round_weights(act, i, t + 2)
                        if engine == "scalar":
                            evacuation(act, i, t)

                with act.Fori(0, turns) as i:
                    turn(i, 4, 4)
                turn(turns, rest, rest - 2)

            @block.vector
            def _(dve):
                split.rest_of_weights(dve, 0, 0)
                split.rest_of_x(dve, rhs)
                split.rest_of_weights(dve, 0, 1)

                def turn(i, count, more):
                    for t in range(count):
                        if t < more:
                            split.rest_of_weights(dve, i, t + 2)
                        if engine == "vector":
                            evacuation(dve, i, t)

                with dve.Fori(0, turns) as i:
                    turn(i, 4, 4)
                turn(turns, rest, rest - 2)


def norm(kit, name, x, tiles, tokens, gain, out, scratch, eps=EPS, shift=None, squares=None):
    ph, ps = kit.ph, kit.ps
    spans = spans_of(tokens)
    squares = out if squares is None else squares
    squared, summed, stepped, rooted, scaled, shifted = (
        ph.sem(f"{name}_{s}") for s in ("squared", "summed", "stepped", "rooted", "scaled", "shifted"))
    with ph as block:
        @block.scalar
        def _(act):
            for j in range(tiles):
                act.activation(squares[:, j, 0:tokens], x[:, j, 0:tokens], ACT.Square).then_inc(squared, 1)
            act.wait_ge(stepped, len(spans))
            act.activation(scratch[:, 0:tokens], scratch[:, 0:tokens], ACT.Sqrt).then_inc(rooted, 1)
            if shift:
                for n, (t0, w) in enumerate(spans):
                    for j in range(tiles):
                        act.wait_ge(scaled, n * tiles + j + 1)
                        act.activation(out[:, j, t0:t0 + w], out[:, j, t0:t0 + w], ACT.Identity,
                                       bias=shift(j, n)).then_inc(shifted, 1)

        @block.tensor
        def _(pe):
            for j in range(tiles):
                pe.wait_ge(squared, j + 1)
                for n, (t0, w) in enumerate(spans):
                    mm = pe.matmul(ps[:, n, 0:w], kit.const("ones"), squares[:, j, t0:t0 + w],
                                   start=(j == 0), stop=(j == tiles - 1))
            mm.then_inc(summed, 1)

        @block.vector
        def _(dve):
            dve.wait_ge(summed, 1)
            for n, (t0, w) in enumerate(spans):
                dve.tensor_scalar(scratch[:, t0:t0 + w], ps[:, n, 0:w], 1.0 / (tiles * P), eps,
                                  ALU.mult, ALU.add).then_inc(stepped, 1)
            dve.wait_ge(rooted, 1)
            dve.reciprocal(scratch[:, 0:tokens], scratch[:, 0:tokens]).then_inc(stepped, 1)
            dve.wait_ge(stepped, len(spans) + 1)
            for n, (t0, w) in enumerate(spans):
                for j in range(tiles):
                    dve.scalar_tensor_tensor(out=out[:, j, t0:t0 + w], in0=x[:, j, t0:t0 + w],
                                             scalar=gain(j, n), in1=scratch[:, t0:t0 + w],
                                             op0=ALU.mult, op1=ALU.mult).then_inc(scaled, 1)


def attention(kit, name, units, p_buf, pt_buf, small, beside=()):
    ph, ps = kit.ph, kit.ps
    n = len(units)
    scored, stepped, maxed, exped, turned, copied, mixed, emitted = (
        ph.sem(f"{name}_{s}") for s in
        ("scored", "stepped", "maxed", "exped", "turned", "copied", "mixed", "emitted"))
    groups = []
    for u, unit in enumerate(units):
        tiles = len(unit["values"])
        for g in range(0, tiles, 4):
            groups.append((u, g, min(4, tiles - g)))
    of_unit = [[g for g in range(len(groups)) if groups[g][0] == u] for u in range(n)]
    exps = []
    for unit in units:
        exps.append((exps[-1] if exps else 0) + (2 if unit["sink"] is not None else 1))

    def keys(unit):
        return P * len(unit["values"])

    def scores(u):
        flat = ps[:, 2 * (u % 2):2 * (u % 2) + 2, :].rearrange("p b n -> p (b n)")
        return flat[:, 0:keys(units[u])]

    def col(u, k):
        c = (u % 4) * 8 + k
        return small[:, c:c + 1]

    with ph as block:
        @block.tensor
        def _(pe):
            def score(u):
                if u >= 2:
                    pe.wait_ge(exped, exps[u - 2])
                for lhs, rhs, width, at in units[u]["scores"]:
                    mm = pe.matmul(scores(u)[:, at:at + width], lhs, rhs, start=True, stop=True)
                mm.then_inc(scored, 1)

            def turn(u):
                pe.wait_ge(exped, exps[u])
                for g in of_unit[u]:
                    _, first, count = groups[g]
                    if g >= 2:
                        pe.wait_ge(copied, g - 1)
                    for k in range(count):
                        c = (first + k) * P
                        mm = pe.transpose(ps[:, 4 + g % 2, k * P:(k + 1) * P],
                                          p_buf[:, u % 2, c:c + P], kit.const("ident"))
                    mm.then_inc(turned, 1)

            def mix(u):
                pe.wait_ge(copied, of_unit[u][-1] + 1)
                if u >= 2:
                    pe.wait_ge(emitted, u - 1)
                values = units[u]["values"]
                for k, v in enumerate(values):
                    mm = pe.matmul(ps[:, 6 + u % 2, 0:v.shape[-1]], pt_buf[:, u % 2, k * P:(k + 1) * P], v,
                                   start=(k == 0), stop=(k == len(values) - 1))
                mm.then_inc(mixed, 1)

            for u in range(n + 2):
                if u < n:
                    score(u)
                if 1 <= u <= n:
                    turn(u - 1)
                if u >= 2:
                    mix(u - 2)

        @block.vector
        def _(dve):
            chain = Chain(dve, stepped)

            def maximum(u):
                unit = units[u]
                dve.wait_ge(scored, u + 1)
                if unit["adjust"]:
                    chain(unit["adjust"](dve, scores(u)))
                chain(dve.reduce_max(col(u, 0), scores(u), AX))
                if unit["sink"] is not None:
                    chain(dve.tensor_tensor(col(u, 0), col(u, 0), unit["sink"], ALU.max))
                dve.tensor_scalar(col(u, 1), col(u, 0), -unit["scale"], None, ALU.mult).then_inc(maxed, 1)

            def emit(u):
                unit = units[u]
                dve.wait_ge(exped, exps[u])
                if unit["sink"] is not None:
                    chain(dve.tensor_tensor(col(u, 2), col(u, 2), col(u, 3), ALU.add))
                chain(dve.reciprocal(col(u, 4), col(u, 2)))
                dve.wait_ge(mixed, u + 1)
                v = unit["values"][0].shape[-1]
                unit["emit"](dve, chain, ps[:, 6 + u % 2, 0:v], col(u, 4)).then_inc(emitted, 1)

            for u in range(n + 2):
                works = beside[u * len(beside) // n:(u + 1) * len(beside) // n]
                if u < n:
                    maximum(u)
                for work in works[0::2]:
                    work(dve)
                if u >= 2:
                    emit(u - 2)
                for work in works[1::2]:
                    work(dve)

        @block.scalar
        def _(act):
            def exponential(u):
                unit = units[u]
                act.wait_ge(maxed, u + 1)
                if u >= 2:
                    act.wait_ge(turned, of_unit[u - 2][-1] + 1)
                act.activation(p_buf[:, u % 2, 0:keys(unit)], scores(u), ACT.Exp, bias=col(u, 1),
                               scale=unit["scale"], accum_out=col(u, 2)).then_inc(exped, 1)
                if unit["sink"] is not None:
                    act.activation(col(u, 3), unit["sink"], ACT.Exp, bias=col(u, 1)).then_inc(exped, 1)

            def copy(u):
                if u >= 2:
                    act.wait_ge(mixed, u - 1)
                for g in of_unit[u]:
                    _, first, count = groups[g]
                    act.wait_ge(turned, g + 1)
                    act.activation(pt_buf[:, u % 2, first * P:(first + count) * P],
                                   ps[:, 4 + g % 2, 0:count * P], ACT.Copy).then_inc(copied, 1)

            for u in range(n + 1):
                if u < n:
                    exponential(u)
                if u >= 1:
                    copy(u - 1)


def to_channels(kit, name, y_tok, blocks, out, gain=None):
    ph, ps = kit.ph, kit.ps
    turned, taken = ph.sem(f"{name}_turned"), ph.sem(f"{name}_taken")
    with ph as block:
        @block.tensor
        def _(pe):
            for b in range(blocks):
                if b >= 8:
                    pe.wait_ge(taken, b - 7)
                for c in range(4):
                    mm = pe.transpose(ps[:, b % 8, c * P:(c + 1) * P], y_tok[:, b, c * P:(c + 1) * P],
                                      kit.const("ident"))
                mm.then_inc(turned, 1)

        @block.vector
        def _(dve):
            for b in range(blocks):
                dve.wait_ge(turned, b + 1)
                for c in range(4):
                    src, dst = ps[:, b % 8, c * P:(c + 1) * P], out[:, c, b * P:(b + 1) * P]
                    if gain:
                        op = dve.tensor_scalar(dst, src, gain(c), None, ALU.mult)
                    else:
                        op = dve.tensor_copy(dst, src)
                op.then_inc(taken, 1)


IN_COLS = 5280
N_Q, N_K, N_V, N_U, N_CQ = 0, 4, 5, 6, 14
AT_CKV, AT_KPE, AT_GATES = 2048, 2176, 2208
WINDOW, SWA_HEADS, MLA_HEADS, TAPS = 128, 8, 8, 31
BLOCKS = SEQ // P
PACK1 = [("g_mix", 8), ("g_mlp", 8), ("g_q", 2), ("g_kv", 1), ("b_dw", 4), ("g_ln", 4), ("b_ln", 4),
         ("taps", 4 * TAPS), ("sinks", SWA_HEADS)]
PACK1_AT = {n: sum(w for _, w in PACK1[:i]) for i, (n, _) in enumerate(PACK1)}
PACK1_WIDTH = sum(w for _, w in PACK1)
THRESHOLDS = list(range(1, 17)) + [math.ceil(16 * 2 ** (3 * j / 16)) for j in range(1, 16)]


def window_bias(kit, pos_skewed, pos_column, rel_bias, bias_dram, fill, finish):
    nc, ph = kit.nc, kit.ph
    n_at = BLOCKS * P
    with ExitStack() as ctx:
        def sb(name, shape, dt=F32):
            return ctx.enter_context(nc.sbuf_tensor(name, shape, dt))

        keys_i, query_i = sb("keys_i", [P, n_at], I32), sb("query_i", [P, BLOCKS], I32)
        dist, reached = sb("dist", [P, n_at]), sb("reached", [P, 2, n_at])
        query, table = sb("query", [P, BLOCKS]), sb("table", [P, 32, SWA_HEADS])
        step = sb("step", [P, 31, SWA_HEADS])
        bias = sb("bias_by_distance", [P, SWA_HEADS, n_at])
        masked = sb("masked", [P, 2 * P])
        loaded, stepped, started, filled, stored = (
            ph.sem(s) for s in ("bias_loaded", "bias_stepped", "bias_started", "bias_filled", "bias_stored"))
        with ph as block:
            @block.sync
            def _(sp):
                sp.dma_start(keys_i[:, :], pos_skewed).then_inc(loaded, 16)
                sp.dma_start(query_i[:, :], pos_column).then_inc(loaded, 16)
                sp.dma_start(table[:, :, :], rel_bias).then_inc(loaded, 16)
                sp.wait_ge(loaded, 48)

            @block.scalar
            def _(act):
                act.wait_ge(started, 1)
                for b in range(BLOCKS):
                    for h in range(SWA_HEADS):
                        act.dma_start(bias_dram[b, h], masked[:, :]).then_inc(filled, 16)

            fill(block)

            @block.sync
            def _(sp):
                sp.wait_ge(filled, 16 * BLOCKS * SWA_HEADS)
                sp.wait_ge(started, 2)
                for b in range(BLOCKS):
                    for h in range(SWA_HEADS):
                        row = bass.AP(bias_dram.tensor, bias_dram[b, h].offset + 1,
                                      [[2 * P + 1, P], [1, P]])
                        sp.dma_start(row, bias[:, h, b * P:(b + 1) * P]).then_inc(stored, 16)
                sp.wait_ge(stored, 16 * BLOCKS * SWA_HEADS)

            @block.vector
            def _(dve):
                dve.memset(masked[:, :], MASKED).then_inc(started, 1)
                chain = Chain(dve, stepped)
                dve.wait_ge(loaded, 48)
                chain(dve.tensor_copy(dist[:, :], keys_i[:, :]))
                chain(dve.tensor_copy(query[:, :], query_i[:, :]))
                dve.tensor_tensor(step[:, :, :], table[:, 1:32, :], table[:, 0:31, :], ALU.subtract)
                for b in range(BLOCKS):
                    d = dist[:, b * P:(b + 1) * P]
                    last = dve.tensor_scalar(d, d, query[:, b:b + 1], -1.0, ALU.subtract, ALU.mult)
                chain(last)
                for h in range(SWA_HEADS):
                    last = dve.tensor_scalar(bias[:, h, :], dist[:, :], 0.0, table[:, 0, h:h + 1],
                                             ALU.mult, ALU.add)
                chain(last)
                for j, at in enumerate(THRESHOLDS):
                    chain(dve.tensor_scalar(reached[:, j % 2, :], dist[:, :], float(at), None, ALU.is_ge))
                    for h in range(SWA_HEADS):
                        last = dve.scalar_tensor_tensor(out=bias[:, h, :], in0=reached[:, j % 2, :],
                                                        scalar=step[:, j, h:h + 1], in1=bias[:, h, :],
                                                        op0=ALU.mult, op1=ALU.add)
                chain(last)
                for h in range(SWA_HEADS):
                    last = dve.tensor_tensor(bias[:, h, 0:P], bias[:, h, 0:P], kit.const("no_prev"), ALU.add)
                last.then_inc(started, 1)

            finish(block)


def rope_tables(kit, positions, cos, sin):
    nc, ph = kit.nc, kit.ph
    rows = slice(64, 96)
    magic = 1.5 * 2.0 ** 23
    parts = [6.28125, 0.0019350051879882812, 3.0199159819e-07]
    with ExitStack() as ctx:
        pos_i = ctx.enter_context(nc.sbuf_tensor("pos_i", [P, SEQ], I32))
        angle, turns, shifted = (ctx.enter_context(nc.sbuf_tensor(n, [P, SEQ], F32))
                                 for n in ("angle", "turns", "shifted"))
        loaded, stepped, reduced, looked_up = (
            ph.sem(s) for s in ("rope_loaded", "rope_stepped", "rope_reduced", "rope_looked_up"))
        with ph as block:
            @block.sync
            def _(sp):
                sp.dma_start(pos_i[rows, :], positions).then_inc(loaded, 16)

            @block.vector
            def _(dve):
                chain = Chain(dve, stepped)
                dve.wait_ge(loaded, 16)
                chain(dve.tensor_copy(angle[rows, :], pos_i[rows, :]))
                chain(dve.tensor_scalar(angle[rows, :], angle[rows, :], kit.const("mla_freq", rows), None, ALU.mult))
                for quarter, out in ((0.0, sin), (0.25, cos)):
                    chain(dve.tensor_scalar(turns[rows, :], angle[rows, :], 1.0 / (2 * math.pi), quarter,
                                            ALU.mult, ALU.add))
                    chain(dve.tensor_scalar(turns[rows, :], turns[rows, :], magic, None, ALU.add))
                    chain(dve.tensor_scalar(turns[rows, :], turns[rows, :], magic, None, ALU.subtract))
                    chain(dve.scalar_tensor_tensor(out=out[rows, :], in0=turns[rows, :], scalar=-parts[0],
                                                   in1=angle[rows, :], op0=ALU.mult, op1=ALU.add))
                    chain(dve.scalar_tensor_tensor(out=out[rows, :], in0=turns[rows, :], scalar=-parts[1],
                                                   in1=out[rows, :], op0=ALU.mult, op1=ALU.add))
                    chain(dve.scalar_tensor_tensor(out=out[rows, :], in0=turns[rows, :], scalar=-parts[2],
                                                   in1=out[rows, :], op0=ALU.mult, op1=ALU.add))
                    chain(dve.tensor_scalar(out[rows, :], out[rows, :], quarter * 2 * math.pi, math.pi,
                                            ALU.add, ALU.min))
                    dve.tensor_scalar(out[rows, :], out[rows, :], -math.pi, None, ALU.max).then_inc(reduced, 1)

            @block.scalar
            def _(act):
                for n, out in enumerate((sin, cos)):
                    act.wait_ge(reduced, n + 1)
                    act.activation(out[rows, :], out[rows, :], ACT.Sin).then_inc(looked_up, 1)


def window_attention(kit, proj, pack, bias_dram, y, u, y_conv):
    nc, ph, ps = kit.nc, kit.ph, kit.ps
    with ExitStack() as ctx:
        def sb(name, shape):
            return ctx.enter_context(nc.sbuf_tensor(name, shape, F32))

        keys = [sb("keys", [P, P + SEQ]), sb("keys_swapped", [P, P + SEQ])]
        values = sb("window_values", [P, BLOCKS + 1, P])
        bias = sb("window_bias", [P, BLOCKS, SWA_HEADS, 2 * P])
        ring = kit.ring
        y_tok = ring[:, 0:BLOCKS * SEQ].rearrange("p (b n) -> p b n", b=BLOCKS)
        p_buf, pt_buf = (ring[:, at:at + 512].rearrange("p (u n) -> p u n", u=2) for at in (2048, 2560))
        small = ring[:, 3072:3104]
        loaded, turned, copied, gated = (ph.sem(s) for s in ("bias_read", "v_turned", "window_copied", "conv_gated"))
        with ph as block:
            @block.sync
            def _(sp):
                for b in range(BLOCKS):
                    sp.dma_start(bias[:, b, :, :], bias_dram[b].rearrange("h q k -> q h k")).then_inc(loaded, 16)
                sp.wait_ge(loaded, 16 * BLOCKS)

            @block.tensor
            def _(pe):
                for b in range(BLOCKS):
                    mm = pe.transpose(ps[:, 0, b * P:(b + 1) * P], proj[:, N_V, b * P:(b + 1) * P],
                                      kit.const("ident"))
                mm.then_inc(turned, 1)

            @block.vector
            def _(dve):
                for kb in keys:
                    dve.memset(kb[:, 0:P], 0.0)
                dve.memset(values[:, 0, :], 0.0)
                dve.tensor_copy(keys[0][:, P:], proj[:, N_K, :])
                dve.wait_ge(turned, 1)
                dve.tensor_copy(values[:, 1:, :].rearrange("p b n -> p (b n)"), ps[:, 0, :])
                dve.memset(u[:, :, 0:TAPS - 1], 0.0)
                for c in range(4):
                    dve.wait_ge(gated, c + 1)
                    dve.tensor_tensor(u[:, c, TAPS - 1:], proj[:, N_U + c, :], proj[:, N_U + 4 + c, :], ALU.mult)

            @block.scalar
            def _(act):
                act.activation(keys[1][0:64, P:], proj[64:128, N_K, :], ACT.Copy)
                act.activation(keys[1][64:128, P:], proj[0:64, N_K, :], ACT.Copy).then_inc(copied, 1)
                for c in range(4):
                    act.activation(proj[:, N_U + 4 + c, :], proj[:, N_U + 4 + c, :], ACT.Sigmoid).then_inc(gated, 1)

        units = []
        for b in range(BLOCKS):
            for h in range(SWA_HEADS):
                kv, half = h // 4, slice(64 * (h % 2), 64 * (h % 2) + 64)
                kb = keys[0] if kv == h % 2 else keys[1]

                def adjust(dve, s, b=b, h=h):
                    return dve.scalar_tensor_tensor(out=s, in0=s, scalar=0.125, in1=bias[:, b, h, :],
                                                    op0=ALU.mult, op1=ALU.add)

                def emit(dve, chain, product, inverse, b=b, h=h):
                    return dve.tensor_scalar(y_tok[:, b, h * 64:(h + 1) * 64], product, inverse, None, ALU.mult)

                units.append(dict(
                    scores=[(proj[half, N_Q + h // 2, b * P:(b + 1) * P], kb[half, b * P:(b + 2) * P], 2 * P, 0)],
                    adjust=adjust, scale=1.0, sink=pack("sinks", h),
                    values=[values[:, b + n, kv * 64:(kv + 1) * 64] for n in range(2)], emit=emit))
        attention(kit, "window", units, p_buf, pt_buf, small, conv_taps(kit, pack, u, y_conv, 0, TAPS // 2 + 1))
        to_channels(kit, "window_y", y_tok, BLOCKS, y)


def conv_taps(kit, pack, u, y, first, last):
    tapped = kit.ph.sem("conv_tapped")

    def work(t, c):
        n = (t - first) * 4 + c
        tap, src = pack("taps", c * TAPS + t), u[:, c, t:t + SEQ]

        def run(dve):
            if n >= 4:
                dve.wait_ge(tapped, n - 3)
            if t == 0:
                op = dve.tensor_scalar(y[:, c, :], src, tap, pack("b_dw", c), ALU.mult, ALU.add)
            else:
                op = dve.scalar_tensor_tensor(out=y[:, c, :], in0=src, scalar=tap, in1=y[:, c, :],
                                              op0=ALU.mult, op1=ALU.add)
            op.then_inc(tapped, 1)
        return run

    return [work(t, c) for t in range(first, last) for c in range(4)]


def conv_finish(kit, pack, y):
    nc, ph, ps = kit.nc, kit.ph, kit.ps
    with ExitStack() as ctx:
        sq = ctx.enter_context(nc.sbuf_tensor("conv_squares", [P, 4, SEQ], F32))
        stat = ctx.enter_context(nc.sbuf_tensor("conv_stat", [P, 2, SEQ], F32))
        summed, stepped, rooted, squared, normed = (
            ph.sem(f"conv_{s}") for s in ("summed", "stepped", "rooted", "squared", "normed"))
        with ph as block:
            @block.scalar
            def _(act):
                for c in range(4):
                    act.wait_ge(normed, c + 1)
                    act.activation(sq[:, c, :], y[:, c, :], ACT.Square).then_inc(squared, 1)
                act.wait_ge(normed, 5)
                act.activation(stat[:, 1, :], stat[:, 1, :], ACT.Sqrt).then_inc(rooted, 1)
                for c in range(4):
                    act.wait_ge(normed, 6 + c)
                    act.activation(sq[:, c, :], y[:, c, :], ACT.Sigmoid,
                                   bias=pack("b_ln", c)).then_inc(squared, 1)

            @block.tensor
            def _(pe):
                for c in range(4):
                    mm = pe.matmul(ps[:, 0, :], kit.const("ones"), y[:, c, :], start=(c == 0), stop=(c == 3))
                mm.then_inc(summed, 1)
                for c in range(4):
                    pe.wait_ge(squared, c + 1)
                    mm = pe.matmul(ps[:, 1, :], kit.const("ones"), sq[:, c, :], start=(c == 0), stop=(c == 3))
                mm.then_inc(summed, 1)

            @block.vector
            def _(dve):
                chain = Chain(dve, stepped)
                dve.wait_ge(summed, 1)
                chain(dve.tensor_scalar(stat[:, 0, :], ps[:, 0, :], 1.0 / SEQ, None, ALU.mult))
                for c in range(4):
                    dve.tensor_tensor(y[:, c, :], y[:, c, :], stat[:, 0, :], ALU.subtract).then_inc(normed, 1)
                dve.wait_ge(summed, 2)
                dve.tensor_scalar(stat[:, 1, :], ps[:, 1, :], 1.0 / SEQ, EPS, ALU.mult, ALU.add).then_inc(normed, 1)
                dve.wait_ge(rooted, 1)
                chain(dve.reciprocal(stat[:, 1, :], stat[:, 1, :]))
                for c in range(4):
                    dve.scalar_tensor_tensor(out=y[:, c, :], in0=y[:, c, :], scalar=pack("g_ln", c),
                                             in1=stat[:, 1, :], op0=ALU.mult, op1=ALU.mult).then_inc(normed, 1)
                for c in range(4):
                    dve.wait_ge(squared, 5 + c)
                    dve.scalar_tensor_tensor(out=y[:, c, :], in0=y[:, c, :], scalar=pack("b_ln", c),
                                             in1=sq[:, c, :], op0=ALU.add, op1=ALU.mult)


def latent_attention(kit, proj, h, pack, w_in, w_q_up, w_kv_up, cos, sin, y, u, y_conv):
    nc, ph, ps = kit.nc, kit.ph, kit.ps
    rope = slice(64, 96)
    with ExitStack() as ctx:
        def sb(name, shape):
            return ctx.enter_context(nc.sbuf_tensor(name, shape, F32))

        latent = sb("latent", [P, 1, SEQ])
        scratch = sb("latent_norm", [P, SEQ])
        queries, keys = sb("latent_q", [P, MLA_HEADS, SEQ]), sb("latent_k", [P, MLA_HEADS, SEQ])
        values = sb("latent_v", [P, BLOCKS, SEQ])
        ring = kit.ring
        w_lat = ring[:, 0:1280].rearrange("p (k n) -> p k n", k=KD)
        w_q = ring[:, 1280:2816].rearrange("p (k n) -> p k n", k=2)
        w_kv = ring[:, 2816:3840]
        turned_part = ring[:, 3840:3840 + SEQ * MLA_HEADS].rearrange("p (h n) -> p h n", h=MLA_HEADS)
        loaded, summed, taken = (ph.sem(s) for s in ("lat_loaded", "lat_summed", "lat_taken"))
        with ph as block:
            @block.sync
            def _(sp):
                sp.dma_start(w_lat, w_in[:, :, AT_CKV:AT_GATES]).then_inc(loaded, 16)
                sp.dma_start(w_q, w_q_up).then_inc(loaded, 16)
                sp.dma_start(w_kv, w_kv_up).then_inc(loaded, 16)
                sp.wait_ge(loaded, 48)

            @block.tensor
            def _(pe):
                pe.wait_ge(loaded, 48)
                for k in range(KD):
                    pe.matmul(ps[:, 0, :], w_lat[:, k, 0:P], h[:, k, :], start=(k == 0), stop=(k == KD - 1))
                for k in range(KD):
                    mm = pe.matmul(ps[rope, 1, :], w_lat[:, k, P:P + 32], h[:, k, :],
                                   start=(k == 0), stop=(k == KD - 1))
                mm.then_inc(summed, 1)

            @block.scalar
            def _(act):
                act.wait_ge(summed, 1)
                act.activation(latent[:, 0, :], ps[:, 0, :], ACT.Copy)
                act.activation(keys[rope, 0, :], ps[rope, 1, :], ACT.Copy).then_inc(taken, 1)

        norm(kit, "q_latent", proj[:, N_CQ:N_CQ + 2, :], 2, SEQ, lambda j, n: pack("g_q", j),
             y[:, 0:2, :], scratch)
        norm(kit, "kv_latent", latent, 1, SEQ, lambda j, n: pack("g_kv", 0), y[:, 2:3, :], scratch)

        summed, taken = ph.sem("up_summed"), ph.sem("up_taken")
        with ph as block:
            @block.tensor
            def _(pe):
                n = 0
                for hd in range(MLA_HEADS):
                    for part in range(2):
                        if n >= 4:
                            pe.wait_ge(taken, n - 3)
                        if part == 0:
                            for k in range(2):
                                mm = pe.matmul(ps[0:96, n % 4, :], w_q[:, k, 96 * hd:96 * (hd + 1)], y[:, k, :],
                                               start=(k == 0), stop=(k == 1))
                        else:
                            mm = pe.matmul(ps[0:64, n % 4, :], w_kv[:, P * hd:P * hd + 64], y[:, 2, :],
                                           start=True, stop=True)
                        mm.then_inc(summed, 1)
                        n += 1
                for b in range(BLOCKS):
                    mm = pe.matmul(ps[:, 4 + b, :], y[:, 2, b * P:(b + 1) * P],
                                   w_kv.rearrange("p (h c) -> p h c", c=P)[:, :, 64:P], start=True, stop=True)
                    mm.then_inc(summed, 1)

            @block.scalar
            def _(act):
                for n in range(2 * MLA_HEADS):
                    act.wait_ge(summed, n + 1)
                    rows, dst = (slice(0, 96), queries) if n % 2 == 0 else (slice(0, 64), keys)
                    act.activation(dst[rows, n // 2, :], ps[rows, n % 4, :], ACT.Copy).then_inc(taken, 1)
                for b in range(BLOCKS):
                    act.wait_ge(summed, 2 * MLA_HEADS + b + 1)
                    act.activation(values[:, b, :], ps[:, 4 + b, :], ACT.Copy).then_inc(taken, 1)

        summed, stepped, timed, cosined, shared = (
            ph.sem(s) for s in ("rot_summed", "rot_stepped", "rot_timed", "rot_cosined", "rot_shared"))
        with ph as block:
            @block.tensor
            def _(pe):
                for n in range(MLA_HEADS + 1):
                    if n == MLA_HEADS:
                        pe.wait_ge(timed, 1)
                    src = queries[rope, n, :] if n < MLA_HEADS else keys[rope, 0, :]
                    pe.matmul(ps[rope, n % 8, :], kit.const("mla_rot", rope), src,
                              start=True, stop=True).then_inc(summed, 1)

            @block.gpsimd
            def _(pool):
                pool.wait_ge(summed, MLA_HEADS + 1)
                for n in range(MLA_HEADS + 1):
                    x = queries[rope, n, :] if n < MLA_HEADS else keys[rope, 0, :]
                    pool.tensor_tensor(x, x, cos[rope, :], ALU.mult).then_inc(cosined, 1)

            @block.vector
            def _(dve):
                for n in range(MLA_HEADS):
                    dve.wait_ge(summed, n + 1)
                    dve.tensor_tensor(turned_part[rope, n, :], ps[rope, n, :], sin[rope, :], ALU.mult).then_inc(timed, 1)
                for n in range(MLA_HEADS):
                    dve.wait_ge(timed, n + 1)
                    dve.wait_ge(cosined, n + 1)
                    last = dve.tensor_tensor(queries[rope, n, :], queries[rope, n, :], turned_part[rope, n, :], ALU.add)
                last.then_inc(stepped, 1)
                dve.wait_ge(stepped, 1)
                dve.wait_ge(summed, MLA_HEADS + 1)
                dve.tensor_tensor(turned_part[rope, 0, :], ps[rope, 0, :], sin[rope, :], ALU.mult).then_inc(timed, 1)
                dve.wait_ge(timed, MLA_HEADS + 1)
                dve.wait_ge(cosined, MLA_HEADS + 1)
                dve.tensor_tensor(keys[rope, 0, :], keys[rope, 0, :], turned_part[rope, 0, :], ALU.add).then_inc(shared, 1)

            @block.scalar
            def _(act):
                act.wait_ge(shared, 1)
                for n in range(1, MLA_HEADS):
                    act.activation(keys[rope, n, :], keys[rope, 0, :], ACT.Copy)

        scale = 96.0 ** -0.5
        p_buf = ring[:, 0:1024].rearrange("p (u n) -> p u n", u=2)
        pt_buf = ring[:, 1024:2048].rearrange("p (u n) -> p u n", u=2)
        small = ring[:, 2048:2080]
        y_tok = ring[:, 2080:2080 + BLOCKS * SEQ].rearrange("p (b n) -> p b n", b=BLOCKS)
        units = []
        for b in range(BLOCKS):
            for hd in range(MLA_HEADS):
                def adjust(dve, s, b=b):
                    diagonal = s[:, b * P:(b + 1) * P]
                    return dve.tensor_tensor(diagonal, diagonal, kit.const("causal"), ALU.add)

                def emit(dve, chain, product, inverse, b=b, hd=hd):
                    return dve.tensor_scalar(y_tok[:, b, hd * 64:(hd + 1) * 64], product, inverse, None, ALU.mult)

                units.append(dict(
                    scores=[(queries[0:96, hd, b * P:(b + 1) * P], keys[0:96, hd, 0:(b + 1) * P], (b + 1) * P, 0)],
                    adjust=adjust, scale=scale, sink=None,
                    values=[values[:, n, hd * 64:(hd + 1) * 64] for n in range(b + 1)], emit=emit))
        attention(kit, "latent", units, p_buf, pt_buf, small, conv_taps(kit, pack, u, y_conv, TAPS // 2 + 1, TAPS))
        to_channels(kit, "latent_y", y_tok, BLOCKS, y)


def merge_branches(kit, h, ys, h_hi, ys_hi, w_in, w_branch, merged, gate, product):
    nc, ph, ps = kit.nc, kit.ph, kit.ps
    branches, kb = 3, 4
    kw = KD + kb
    units, turns = 2 * branches, D_MODEL // 256
    part = 2 * kw * P
    w_hi, w_lo = (nc.alloc_sbuf_tensor_at(f"merge_w{n}", [P, 2, kw, P], F32R, offset=kit.ring_at + n * part * 4)
                  for n in range(2))
    raw = kit.ring[:, 2 * part:3 * part].rearrange("p (s k n) -> p s k n", s=2, k=kw)
    landed = [ph.sem(f"merge_landed{s}") for s in range(2)]
    w_rounded, w_ready, x_rounded, x_cut, x_ready, summed, gated, timed, added = (ph.sem(f"merge_{s}") for s in (
        "w_rounded", "w_ready", "x_rounded", "x_cut", "x_ready", "summed", "gated", "timed", "added"))
    with ExitStack() as ctx:
        h_lo = ctx.enter_context(nc.sbuf_tensor("merge_h_lo", [P, KD, SEQ], F32R))
        ys_lo = [ctx.enter_context(nc.sbuf_tensor(f"merge_y_lo{s}", [P, kb, SEQ], F32R)) for s in range(branches)]
        xs = [(h[:, k, :], h_hi[:, k, :], h_lo[:, k, :]) for k in range(KD)]
        for s in range(branches):
            xs += [(ys[s][:, k, :], ys_hi[s][:, k, :], ys_lo[s][:, k, :]) for k in range(kb)]

        with ph as block:
            @block.sync
            def _(sp):
                def load(i, u):
                    t, s = u // branches, u % branches
                    sp.dma_start(raw[:, u % 2, 0:KD, :], w_in[:, :, bass.ds(i * 256 + (AT_GATES + s * D_MODEL + t * P), P)])\
                        .then_inc(landed[u % 2], 16)
                    sp.dma_start(raw[:, u % 2, KD:, :], w_branch[:, s * kb:(s + 1) * kb, bass.ds(i * 256 + t * P, P)])\
                        .then_inc(landed[u % 2], 16)

                def turn(i, first):
                    for u in range(units):
                        if not first or u >= 2:
                            sp.wait_ge(w_ready, i * units + (u - 1))
                        load(i, u)

                turn(0, True)
                with sp.Fori(1, turns) as i:
                    turn(i, False)

            @block.tensor
            def _(pe):
                def turn(i, first):
                    for u in range(units):
                        s, bank = u % branches, u % 3
                        pe.wait_ge(w_ready, i * units + (u + 1))
                        if not first or u >= 3:
                            pe.wait_ge(timed, i * units + (u - 2))
                        for k in range(kw):
                            n = k if k < KD else KD + s * kb + k - KD
                            if first and u < branches and (u == 0 or k >= KD):
                                pe.wait_ge(x_ready, n + 1)
                            _, hi, lo = xs[n]
                            out = ps[:, bank if k < KD else 4 + bank, :]
                            for m, (w, x) in enumerate(((w_hi, hi), (w_hi, lo), (w_lo, hi))):
                                mm = pe.matmul(out, w[:, u % 2, k, :], x, start=(k in (0, KD) and m == 0),
                                               stop=(k in (KD - 1, kw - 1) and m == 2))
                        mm.then_inc(summed, 1)

                turn(0, True)
                with pe.Fori(1, turns) as i:
                    turn(i, False)

            @block.scalar
            def _(act):
                def weights(i, u):
                    act.wait_ge(landed[u % 2], i * 96 + (u // 2 + 1) * 32)
                    act.activation(w_hi[:, u % 2], raw[:, u % 2], ACT.Copy).then_inc(w_rounded, 1)

                def keep_high(n):
                    act.wait_ge(x_cut, n + 1)
                    act.activation(xs[n][1], xs[n][0], ACT.Copy).then_inc(x_ready, 1)

                weights(0, 0)
                for n, (x, hi, lo) in enumerate(xs):
                    act.activation(lo, x, ACT.Copy).then_inc(x_rounded, 1)
                    if n > 0:
                        keep_high(n - 1)
                    if n == kw:
                        weights(0, 1)
                keep_high(len(xs) - 1)

                def turn(i, first, last):
                    for u in range(units):
                        act.wait_ge(summed, i * units + (u + 1))
                        if not last or u < units - 2:
                            weights(i, u + 2)
                        if not first or u >= 3:
                            act.wait_ge(timed, i * units + (u - 2))
                        act.activation(gate[:, u % 3, :], ps[:, u % 3, :], ACT.Sigmoid).then_inc(gated, 1)

                turn(0, True, False)
                with act.Fori(1, turns - 1) as i:
                    turn(i, False, False)
                turn(turns - 1, False, True)

            @block.vector
            def _(dve):
                def weights(i, u):
                    dve.wait_ge(w_rounded, i * units + (u + 1))
                    dve.tensor_tensor(w_lo[:, u % 2], raw[:, u % 2], w_hi[:, u % 2].bitcast(F32), ALU.subtract)\
                        .then_inc(w_ready, 1)

                weights(0, 0)
                for n, (x, hi, lo) in enumerate(xs):
                    dve.wait_ge(x_rounded, n + 1)
                    dve.tensor_tensor(lo, x, lo.bitcast(F32), ALU.subtract).then_inc(x_cut, 1)
                    if n == kw:
                        weights(0, 1)

                def turn(i, last):
                    for u in range(units):
                        if not last or u < units - 2:
                            weights(i, u + 2)
                        t, s = u // branches, u % branches
                        dve.wait_ge(gated, i * units + (u + 1))
                        total = merged[:, bass.ds((i * 2 + t) * SEQ, SEQ)]
                        out = total if s == 0 else product[:, s % 2, :]
                        dve.tensor_tensor(out, gate[:, u % 3, :], ps[:, 4 + u % 3, :], ALU.mult).then_inc(timed, 1)
                        if s > 0:
                            dve.wait_ge(timed, i * units + (u + 1))
                            if s > 1:
                                dve.wait_ge(added, i * 4 + (2 * t + 1))
                            dve.tensor_tensor(total, total, product[:, s % 2, :], ALU.add).then_inc(added, 1)

                with dve.Fori(0, turns - 1) as i:
                    turn(i, False)
                turn(turns - 1, True)


def layer_rows(w, layer):
    return w[bass.ds(layer, 1), :, :].rearrange("a (k p) n -> p (a k) n", p=P)


def first_block(kit, x, d, bias_dram):
    nc, ph = kit.nc, kit.ph
    with ExitStack() as ctx:
        def sb(name, shape):
            return ctx.enter_context(nc.sbuf_tensor(name, shape, F32))

        pack_sb = sb("pack1", [P, PACK1_WIDTH])
        cos, sin = sb("rope_cos", [P, SEQ]), sb("rope_sin", [P, SEQ])
        h_whole, (h_hi,) = kit.shared(ctx, "normed", [P, KD, SEQ], [("normed_hi", [KD, SEQ])])
        h = h_whole[:, :, :]
        rope_tables(kit, d["positions"], cos, sin)

        def pack(name, n):
            at = PACK1_AT[name] + n
            return pack_sb[:, at:at + 1]

        with nc.Fori(0, DEPTH) as layer:
            loaded = ph.sem("pack_loaded")
            with ph as block:
                @block.sync
                def _(sp):
                    sp.dma_start(pack_sb[:, :], d["pack1"][bass.ds(layer, 1)].rearrange("a p n -> (a p) n"))\
                        .then_inc(loaded, 16)
                    sp.wait_ge(loaded, 16)

            w_in, w_branch, w_out, w_up, w_down = (
                layer_rows(d[n], layer) for n in ("w_in", "w_branch", "w_out", "w_up", "w_down"))
            w_q_up = layer_rows(d["w_q_up"], layer)
            w_kv_up = d["w_kv_up"][bass.ds(layer, 1)].rearrange("a k n -> (a k) n")
            with ExitStack() as mixing:
                def mb(name, shape):
                    return mixing.enter_context(nc.sbuf_tensor(name, shape, F32))

                ys, ys_hi = [], []
                for n in range(3):
                    whole, (hi,) = kit.shared(mixing, f"branch{n}", [P, 4, SEQ], [(f"branch{n}_hi", [4, SEQ])])
                    ys.append(whole[:, :, :])
                    ys_hi.append(hi)
                norm(kit, "mix_norm", x, KD, SEQ, lambda j, n: pack("g_mix", j), h, ys[0].rearrange("p k n -> p (k n)"))
                with nc.sbuf_tensor("projected", [P, 16, SEQ], F32) as proj:
                    flat = proj[:, :, :].rearrange("p k n -> p (k n)")
                    gemm(kit, "project", w_in, 2048, h, SEQ,
                         lambda act, j, banks: act.activation(flat[:, bass.ds(j * SEQ, SEQ)], banks[0], ACT.Copy))
                    with nc.sbuf_tensor("conv_in", [P, 4, TAPS - 1 + SEQ], F32) as u:
                        window_attention(kit, proj, pack, bias_dram, ys[0], u, ys[1])
                        latent_attention(kit, proj, h, pack, w_in, w_q_up, w_kv_up, cos, sin, ys[2], u, ys[1])
                    conv_finish(kit, pack, ys[1])
                with ExitStack() as merging:
                    merged = merging.enter_context(nc.sbuf_tensor("merged", [P, KD * SEQ], F32))
                    gate = merging.enter_context(nc.sbuf_tensor("gate", [P, 3, SEQ], F32))
                    product = merging.enter_context(nc.sbuf_tensor("gated", [P, 2, SEQ], F32))
                    merge_branches(kit, h, ys, h_hi, ys_hi, w_in, w_branch, merged, gate, product)
                    m = merged[:, :].rearrange("p (k n) -> p k n", k=KD)

                    def add_to_x(dve, j, banks):
                        at = x[:, bass.ds(j, 1), :].rearrange("p a n -> p (a n)")
                        return dve.tensor_tensor(at, at, banks[0], ALU.add)

                    gemm(kit, "mix_out", w_out, D_MODEL, m, SEQ, add_to_x, engine="vector")
            norm(kit, "mlp_norm", x, KD, SEQ, lambda j, n: pack("g_mlp", j), h, kit.ring[:, 0:SEQ])
            mlp(kit, "mlp", w_up, w_down, h, SEQ, add_to_x)
            with ph:
                pass


def mlp(kit, name, w_up, w_down, h, tokens, add_to_x, in_place=None):
    nc, ph, ps = kit.nc, kit.ph, kit.ps
    quarters, up, tiles = D_FF // 1024, 8, 16
    spans = spans_of(tokens)
    room = 4

    def banks(t):
        b = t % room * len(spans)
        return [ps[:, b + s, 0:w] for s, (_, w) in enumerate(spans)]

    with Split(kit, name, tokens, in_place) as split, ExitStack() as ctx:
        def sb(suffix, shape, dtype):
            return ctx.enter_context(nc.sbuf_tensor(f"{name}_{suffix}", shape, dtype))

        hidden_hi, hidden_lo = (sb(n, [P, up, tokens], F32R) for n in ("hidden_hi", "hidden_lo"))
        relu, squares = sb("relu", [P, 2, tokens], F32), sb("squares", [P, tokens], F32)
        summed, relued, squared, rounded, ready, added = (ph.sem(f"{name}_{s}") for s in (
            "summed", "relued", "squared", "hidden_rounded", "hidden_ready", "added"))

        with ph as block:
            @block.sync
            def _(sp):
                def load(q, pair):
                    if pair < 4:
                        split.load(sp, pair, w_up[:, :, bass.ds(q * 1024 + pair * 256, 256)])
                    else:
                        split.load(sp, pair, w_down[:, bass.ds(q * KD, KD), (pair - 4) * 256:(pair - 3) * 256])

                def quarter(q, first):
                    for pair in range(8):
                        if not first or pair >= 2:
                            sp.wait_ge(split.w_ready, q * tiles + (2 * pair - 2))
                        load(q, pair)

                quarter(0, True)
                with sp.Fori(1, quarters) as q:
                    quarter(q, False)

            @block.tensor
            def _(pe):
                def quarter(q, first):
                    for t in range(tiles):
                        if 4 <= t < 12:
                            pe.wait_ge(relued, q * up + (t - 3))
                        elif t >= 12:
                            pe.wait_ge(added, q * up + (t - 11))
                        elif not first:
                            pe.wait_ge(added, q * up + (t - 3))
                        arriving = None
                        if t == 0 and first:
                            arriving = lambda k: pe.wait_ge(split.x_ready, k + 1)
                        if t == up:
                            arriving = lambda k: pe.wait_ge(ready, q * up + (k + 1))
                        x = (split.x_hi, split.x_lo) if t < up else (hidden_hi, hidden_lo)
                        split.multiply(pe, q, t, x, banks(t), spans, tiles, arriving).then_inc(summed, 1)

                quarter(0, True)
                with pe.Fori(1, quarters) as q:
                    quarter(q, False)

            @block.scalar
            def _(act):
                split.round_weights(act, 0, 0, tiles)
                split.round_x(act, h)
                split.round_weights(act, 0, 1, tiles)

                def quarter(q, first, last):
                    for t in range(tiles):
                        act.wait_ge(summed, q * tiles + (t + 1))
                        if not last or t < tiles - 2:
                            split.round_weights(act, q, t + 2, tiles)
                        if t < up:
                            if not first or t >= 2:
                                act.wait_ge(squared, q * up + (t - 1))
                            for (t0, w), bank in zip(spans, banks(t)):
                                ins = act.activation(relu[:, t % 2, t0:t0 + w], bank, ACT.Relu)
                            ins.then_inc(relued, 1)
                            act.wait_ge(relued, q * up + (t + 1))
                            act.activation(hidden_hi[:, t, :], relu[:, t % 2, :], ACT.Square).then_inc(rounded, 1)

                quarter(0, True, False)
                with act.Fori(1, quarters - 1) as q:
                    quarter(q, False, False)
                quarter(quarters - 1, False, True)

            @block.vector
            def _(dve):
                split.rest_of_weights(dve, 0, 0, tiles)
                split.rest_of_x(dve, h)
                split.rest_of_weights(dve, 0, 1, tiles)

                def quarter(q, first, last):
                    for t in range(tiles):
                        if not last or t < tiles - 2:
                            split.rest_of_weights(dve, q, t + 2, tiles)
                        if t < up:
                            if not first or t >= 1:
                                dve.wait_ge(ready, q * up + t)
                            dve.wait_ge(relued, q * up + (t + 1))
                            dve.tensor_tensor(squares[:, :], relu[:, t % 2, :], relu[:, t % 2, :], ALU.mult)\
                                .then_inc(squared, 1)
                            dve.wait_ge(squared, q * up + (t + 1))
                            dve.wait_ge(rounded, q * up + (t + 1))
                            dve.tensor_tensor(hidden_lo[:, t, :], squares[:, :], hidden_hi[:, t, :].bitcast(F32),
                                              ALU.subtract).then_inc(ready, 1)
                        else:
                            if not first:
                                dve.wait_ge(added, q * up + (t - up + 1 - up))
                            dve.wait_ge(summed, q * tiles + (t + 1))
                            add_to_x(dve, t - up, banks(t)).then_inc(added, 1)

                quarter(0, True, False)
                with dve.Fori(1, quarters - 1) as q:
                    quarter(q, False, False)
                quarter(quarters - 1, False, True)


W = CTX + 1 + SEQ
WS = CTX + 2 + SEQ
T2 = CTX + SEQ
EVEN_A, EVEN_B = 1536, 1792
RW_R, RW_K, RW_V, RW_WA, RW_G = 0, 4, 8, 12, 13
DECAY = -math.exp(-0.5)
LAM_INIT = 0.8 - 0.6 * math.exp(0.0)
GN_EPS = 64e-5
PACK2 = [("mod_b0", 48), ("mod_b1", 48), ("n1_0", 8), ("n2_0", 8), ("n1_1", 8), ("n2_1", 8), ("final", 8),
         ("g_final", 8), ("c", 16), ("lam", 4), ("subln", 1), ("mu", 14), ("w0_f", 4), ("w0_b", 4), ("a0", 4),
         ("k_k", 4), ("k_a", 4), ("r_k", 4), ("lnx_w", 4), ("lnx_b", 4), ("conv_w", 40), ("conv_b", 8),
         ("dt_bias", 16), ("a_log", 16), ("d_skip", 4), ("ssm_norm", 4), ("gk_b", 4), ("gla_norm", 1)]
PACK2_AT = {n: sum(w for _, w in PACK2[:i]) for i, (n, _) in enumerate(PACK2)}
PACK2_WIDTH = sum(w for _, w in PACK2)


class Steps:

    def __init__(self, done, *names):
        self.done, self.names, self.i = done, names, None

    def value(self, turn, name):
        return turn * len(self.names) + (self.names.index(name) + 2)

    def before(self, turn):
        return turn * len(self.names) + 1


def over(column_block, n):
    return column_block.unsqueeze(1).broadcast_to([P, n, column_block.shape[-1]])


def along(columns, n):
    return columns.unsqueeze(2).broadcast_to([columns.shape[0], columns.shape[1], n])


def modulation(kit, weights, biases, cvec, rows, mods):
    ph, ps = kit.ph, kit.ps
    width, kt, ring_slots = 512, 4, 4
    groups = 6 * D_MODEL // width
    slot_floats = kt * width
    landed = [ph.sem(f"mod_landed{s}") for s in range(ring_slots)]
    summed, emptied, turned, biased = (ph.sem(f"mod_{s}") for s in ("summed", "emptied", "turned", "biased"))
    slots = [(layer, g, half) for layer in range(2) for g in range(groups) for half in range(2)]

    def slot(n):
        s = n % ring_slots
        return kit.ring[:, s * slot_floats:(s + 1) * slot_floats].rearrange("p (k n) -> p k n", k=kt)

    def fill(block):
        @block.sync
        def _(sp):
            for n, (layer, g, half) in enumerate(slots):
                if n >= ring_slots:
                    sp.wait_ge(summed, n - ring_slots + 1)
                sp.dma_start(slot(n), weights[layer][:, half * kt:(half + 1) * kt, g * width:(g + 1) * width])\
                    .then_inc(landed[n % ring_slots], 16)

        @block.tensor
        def _(pe):
            for n, (layer, g, half) in enumerate(slots):
                pe.wait_ge(landed[n % ring_slots], 16 * (n // ring_slots + 1))
                bank = n // 2
                if half == 0 and bank >= 4:
                    pe.wait_ge(emptied, bank - 3)
                for k in range(kt):
                    mm = pe.matmul(ps[0:2, bank % 4, :], cvec[:, half * kt + k, :], slot(n)[:, k, :],
                                   start=(half == 0 and k == 0), stop=(half == 1 and k == kt - 1))
                mm.then_inc(summed, 1)
            pe.wait_ge(emptied, 2 * groups)
            for layer in range(2):
                for t in range(48):
                    mm = pe.transpose(ps[:, 4 + layer, 2 * t:2 * t + 2], rows[0:2, layer, t * P:(t + 1) * P],
                                      kit.const("ident")[0:2, 0:2])
                mm.then_inc(turned, 1)

        @block.scalar
        def _(act):
            for bank in range(2 * groups):
                act.wait_ge(summed, 2 * bank + 2)
                layer, g = bank // groups, bank % groups
                act.activation(rows[0:2, layer, g * width:(g + 1) * width], ps[0:2, bank % 4, :],
                               ACT.Copy).then_inc(emptied, 1)
            for layer in range(2):
                act.wait_ge(turned, layer + 1)
                act.activation(mods[layer][:, :, :].rearrange("p t n -> p (t n)"), ps[:, 4 + layer, 0:96],
                               ACT.Copy).then_inc(biased, 1)

    def finish(block):
        @block.vector
        def _(dve):
            for layer in range(2):
                dve.wait_ge(biased, layer + 1)
                m = mods[layer][:, :, :]
                dve.tensor_tensor(m, m, along(biases[layer], 2), ALU.add)

    return fill, finish


def modulation_gains(kit, name, mods, gains, g1, g2):
    ph = kit.ph
    stepped = ph.sem(f"{name}_stepped")
    with ph as block:
        @block.vector
        def _(dve):
            for m, (g, at) in enumerate(((g1, 8), (g2, 32))):
                dve.tensor_scalar(gains[:, m, :, :], mods[:, at:at + 8, :], 1.0, None, ALU.add).then_inc(stepped, 1)
                dve.wait_ge(stepped, 2 * m + 1)
                dve.tensor_tensor(gains[:, m, :, :], gains[:, m, :, :], along(g, 2), ALU.mult).then_inc(stepped, 1)


def diff_attention(kit, h, pack2, w_in, axial_dram, y):
    nc, ph, ps = kit.nc, kit.ph, kit.ps
    blocks = T2 // P
    with ExitStack() as ctx:
        def sb(name, shape):
            return ctx.enter_context(nc.sbuf_tensor(name, shape, F32))

        proj = sb("diff_proj", [P, 12, T2])
        flat = proj[:, :, :].rearrange("p k n -> p (k n)")

        def store(act, j, banks):
            for (t0, w), bank in zip(spans_of(T2), banks):
                ins = act.activation(flat[:, bass.ds(j * T2 + t0, w)], bank, ACT.Copy)
            return ins

        gemm(kit, "diff_project", w_in[:, :, 0:EVEN_A], EVEN_A, h, T2, store)
        values, y_tok = sb("diff_values", [P, blocks, 512]), sb("diff_y", [P, blocks, 512])
        lam = sb("lambda", [P, 4])
        squares, mean = sb("diff_squares", [P, P]), sb("diff_mean", [P, 2, 4])
        axial = sb("axial", [P, P + 2 * SEQ])
        rot, cos, sin = axial[:, 0:P], axial[:, P:P + SEQ], axial[:, P + SEQ:]

        turned = kit.ring[:, 0:8 * SEQ].rearrange("p (c n) -> p c n", c=8)
        loaded, rotated, timed, cosined, v_turned, v_taken, lam_stepped, lam_summed, lam_exped = (
            ph.sem(f"diff_{s}") for s in
            ("loaded", "rotated", "timed", "cosined", "v_turned", "v_taken", "lam_stepped", "lam_summed", "lam_exped"))
        with ph as block:
            @block.sync
            def _(sp):
                sp.dma_start(axial[:, :], axial_dram).then_inc(loaded, 16)
                sp.wait_ge(loaded, 16)

            @block.tensor
            def _(pe):
                pe.wait_ge(loaded, 16)
                for c in range(8):
                    if c >= 4:
                        pe.wait_ge(timed, c - 3)
                    pe.matmul(ps[:, c % 4, :], rot, proj[:, c, CTX:], start=True, stop=True).then_inc(rotated, 1)
                pe.wait_ge(lam_stepped, 1)
                pe.matmul(ps[:, 7, 0:2], kit.const("ones"), lam[:, 0:2], start=True, stop=True).then_inc(lam_summed, 1)
                for b in range(blocks):
                    if b >= 3:
                        pe.wait_ge(v_taken, b - 2)
                    for c in range(4):
                        mm = pe.transpose(ps[:, 4 + b % 3, c * P:(c + 1) * P], proj[:, 8 + c, b * P:(b + 1) * P],
                                          kit.const("ident"))
                    mm.then_inc(v_turned, 1)

            @block.gpsimd
            def _(pool):
                pool.wait_ge(loaded, 16)
                for c in range(8):
                    pool.wait_ge(rotated, c + 1)
                    pool.tensor_tensor(proj[:, c, CTX:], proj[:, c, CTX:], cos, ALU.mult).then_inc(cosined, 1)

            @block.vector
            def _(dve):
                dve.wait_ge(loaded, 16)
                at = PACK2_AT["lam"]
                cols = pack2(slice(at, at + 4))
                dve.tensor_tensor(lam[:, 0:2], cols[:, 0:3:2], cols[:, 1:4:2], ALU.mult).then_inc(lam_stepped, 1)
                for c in range(8):
                    dve.wait_ge(rotated, c + 1)
                    dve.tensor_tensor(turned[:, c, :], ps[:, c % 4, :], sin, ALU.mult).then_inc(timed, 1)
                for c in range(8):
                    dve.wait_ge(timed, c + 1)
                    dve.wait_ge(cosined, c + 1)
                    dve.tensor_tensor(proj[:, c, CTX:], proj[:, c, CTX:], turned[:, c, :], ALU.add)
                dve.wait_ge(lam_exped, 1)
                dve.tensor_tensor(lam[:, 0:1], lam[:, 3:4], lam[:, 2:3], ALU.subtract).then_inc(lam_stepped, 1)
                dve.wait_ge(lam_stepped, 2)
                dve.tensor_scalar(lam[:, 0:1], lam[:, 0:1], -LAM_INIT, None, ALU.add)

            @block.scalar
            def _(act):
                act.wait_ge(lam_summed, 1)
                act.activation(lam[:, 2:4], ps[:, 7, 0:2], ACT.Exp).then_inc(lam_exped, 1)
                for b in range(blocks):
                    act.wait_ge(v_turned, b + 1)
                    act.activation(values[:, b, :], ps[:, 4 + b % 3, :], ACT.Copy).then_inc(v_taken, 1)

        p_buf = kit.ring[:, 0:2 * T2].rearrange("p (u n) -> p u n", u=2)
        pt_buf = kit.ring[:, 2 * T2:4 * T2].rearrange("p (u n) -> p u n", u=2)
        small = kit.ring[:, 4 * T2:4 * T2 + 32]
        factor = kit.ring[:, 4 * T2 + 32:4 * T2 + 34]
        units = []
        for b in range(blocks):
            seen = CTX if b < CTX // P else T2
            for hd in range(4):
                for m in range(2):
                    half = slice(64 * m, 64 * m + 64)

                    def emit(dve, chain, product, inverse, b=b, hd=hd, m=m):
                        out = y_tok[:, b, hd * P:(hd + 1) * P]
                        if m == 0:
                            return dve.tensor_scalar(out, product, inverse, None, ALU.mult)
                        chain(dve.tensor_tensor(factor[:, 0:1], inverse, lam[:, 0:1], ALU.mult))
                        return dve.scalar_tensor_tensor(out=out, in0=product, scalar=factor[:, 0:1], in1=out,
                                                        op0=ALU.mult, op1=ALU.add)

                    q = proj[half, hd, b * P:(b + 1) * P]
                    scores = [(q, proj[half, 4 + hd, at:min(at + BANK, seen)], min(BANK, seen - at), at)
                              for at in range(0, seen, BANK)]
                    units.append(dict(
                        scores=scores, adjust=None, scale=0.125, sink=None,
                        values=[values[:, n, hd * P:(hd + 1) * P] for n in range(seen // P)], emit=emit))
        attention(kit, "diff", units, p_buf, pt_buf, small)

        stepped, rooted, normed = (ph.sem(f"diff_{s}") for s in ("stat_stepped", "rooted", "normed"))
        stats = kit.ring[:, 0:4 * blocks]
        with ph as block:
            @block.vector
            def _(dve):
                chain = Chain(dve, stepped)
                for b in range(blocks):
                    for hd in range(4):
                        at = y_tok[:, b, hd * P:(hd + 1) * P]
                        chain(dve.tensor_tensor(squares[:, :], at, at, ALU.mult))
                        chain(dve.tensor_reduce(stats[:, 4 * b + hd:4 * b + hd + 1], squares[:, :], AX, ALU.add))
                dve.tensor_scalar(stats, stats, 1.0 / P, 1e-5, ALU.mult, ALU.add).then_inc(normed, 1)
                dve.wait_ge(rooted, 1)
                chain(dve.reciprocal(stats, stats))
                chain(dve.tensor_scalar(stats, stats, 1.0 - LAM_INIT, None, ALU.mult))
                for b in range(blocks):
                    out = y_tok[:, b, :].rearrange("p (h n) -> p h n", h=4)
                    dve.tensor_tensor(out, out, along(stats[:, 4 * b:4 * b + 4], P), ALU.mult)

            @block.scalar
            def _(act):
                act.wait_ge(normed, 1)
                act.activation(stats, stats, ACT.Sqrt).then_inc(rooted, 1)

        to_channels(kit, "diff_y", y_tok, blocks, y, gain=lambda c: pack2(slice(PACK2_AT["subln"], PACK2_AT["subln"] + 1)))


RW_SPANS = [(0, CTX + 1), (CTX + 1, SEQ)]


def rwkv_prepare(kit, f, w_dram, pack2, cum, kk, b_neg, small_cols):
    nc, ph, ps = kit.nc, kit.ph, kit.ps
    ring = kit.ring
    tmp = [ring[:, n * W:(n + 1) * W] for n in range(4)]
    resets = ring[:, 4 * W:5 * W]
    w2 = ring[:, 5 * W:5 * W + 2048].rearrange("p (m n) -> p m n", m=4)
    def mixed(c):
        return f[:, c, 1:1 + W]

    def col(name, c):
        at = PACK2_AT[name] + c
        return pack2(slice(at, at + 1))

    loaded, shifted, bent, summed, taken, squared, ksummed, stepped, rooted, ones_less = (
        ph.sem(f"rw_{s}") for s in
        ("loaded", "shifted", "bent", "summed", "taken", "squared", "ksummed", "stepped", "rooted", "ones_less"))
    with ph as block:
        @block.sync
        def _(sp):
            for m, (w, rows) in enumerate(((w_dram[0], slice(0, 64)), (w_dram[1], slice(0, 64)),
                                           (w_dram[2], slice(64, 128)))):
                sp.dma_start(w2[rows, m, :], w).then_inc(loaded, 16)
            sp.wait_ge(loaded, 48)

        @block.vector
        def _(dve):
            chain = Chain(dve, stepped)
            for n, c in enumerate((RW_WA, RW_G) + tuple(range(12))):
                t = tmp[n % 2]
                chain(dve.tensor_tensor(t, f[:, c, 0:W], f[:, c, 2:2 + W], ALU.add))
                chain(dve.scalar_tensor_tensor(out=t, in0=t, scalar=0.5, in1=mixed(c), op0=ALU.mult, op1=ALU.subtract))
                dve.scalar_tensor_tensor(out=mixed(c), in0=t, scalar=col("mu", c), in1=mixed(c),
                                         op0=ALU.mult, op1=ALU.add).then_inc(shifted, 1)
            for c in range(4):
                dve.wait_ge(shifted, 2 + RW_K + c + 1)
                dve.tensor_scalar(kk[:, c, :], mixed(RW_K + c), col("k_k", c), None, ALU.mult).then_inc(ones_less, 1)
            at = PACK2_AT["k_a"]
            chain(dve.tensor_scalar(small_cols[:, 0:4], pack2(slice(at, at + 4)), -1.0, 1.0, ALU.mult, ALU.add))
            for c in range(4):
                dve.wait_ge(taken, 3 * (c + 1))
                chain(dve.tensor_scalar(tmp[0], b_neg[:, c, :], col("k_a", c), small_cols[:, c:c + 1],
                                        ALU.mult, ALU.add))
                chain(dve.tensor_tensor(mixed(RW_K + c), mixed(RW_K + c), tmp[0], ALU.mult))
            for c in range(4):
                dve.wait_ge(rooted, c + 1)
                t = tmp[2 + c % 2]
                chain(dve.tensor_scalar(t, t, 1e-12, None, ALU.max))
                chain(dve.reciprocal(t, t))
                chain(dve.tensor_tensor(kk[:, c, :], kk[:, c, :], t, ALU.mult))
                dve.scalar_tensor_tensor(out=b_neg[:, c, :], in0=kk[:, c, :], scalar=-1.0, in1=b_neg[:, c, :],
                                         op0=ALU.mult, op1=ALU.mult).then_inc(squared, 1)
            chain(dve.memset(resets, 1.0))
            for at, n in ((0, CTX // 64), (CTX + 1, SEQ // 64)):
                chain(dve.memset(resets[:, at:at + 64 * n].rearrange("p (n t) -> p n t", t=64)[:, :, 0:1], 0.0))
            for c in range(4):
                for d in range(2):
                    chain(dve.tensor_scalar(cum[d][:, c, :], cum[d][:, c, :], DECAY, None, ALU.mult))
                chain(dve.tensor_tensor_scan(cum[0][:, c, :], resets, cum[0][:, c, :], 0.0, ALU.mult, ALU.add))
                chain(dve.tensor_tensor_scan(tmp[0], resets, cum[1][:, c, :], 0.0, ALU.mult, ALU.add))
                chain(dve.tensor_tensor(cum[1][:, c, :], cum[1][:, c, :], tmp[0], ALU.subtract))
                for at, n in ((0, CTX // 64), (CTX + 1, SEQ // 64)):
                    part = cum[1][:, c, at:at + 64 * n].rearrange("p (n t) -> p n t", t=64)
                    total = tmp[0][:, at:at + 64 * n].rearrange("p (n t) -> p n t", t=64)[:, :, 63:64]
                    chain(dve.tensor_tensor(part, part, total.broadcast_to([P, n, 64]), ALU.add))

        @block.scalar
        def _(act):
            act.wait_ge(shifted, 1)
            act.activation(f[0:64, RW_WA, 1:1 + W], f[0:64, RW_WA, 1:1 + W], ACT.Tanh).then_inc(bent, 1)
            act.wait_ge(shifted, 2)
            act.activation(mixed(RW_G), mixed(RW_G), ACT.Sigmoid)
            n = 0
            for c in range(4):
                for m, (out, bias) in enumerate(((cum[0], "w0_f"), (cum[1], "w0_b"), (b_neg, "a0"))):
                    n += 1
                    act.wait_ge(summed, n)
                    for s, (t0, w) in enumerate(RW_SPANS):
                        ins = act.activation(out[:, c, t0:t0 + w], ps[:, 2 * (n % 3) + s, 0:w], ACT.Sigmoid,
                                             bias=col(bias, c))
                    ins.then_inc(taken, 1)
            for c in range(4):
                act.wait_ge(ones_less, c + 1)
                if c >= 2:
                    act.wait_ge(squared, c - 1)
                    act.wait_ge(rooted, c - 1)
                t = tmp[2 + c % 2]
                act.activation(t, kk[:, c, :], ACT.Square).then_inc(bent, 1)
                act.wait_ge(ksummed, c + 1)
                for s, (t0, w) in enumerate(RW_SPANS):
                    ins = act.activation(t[:, t0:t0 + w], ps[:, 6 + s, 0:w], ACT.Sqrt)
                ins.then_inc(rooted, 1)

        @block.tensor
        def _(pe):
            pe.wait_ge(loaded, 48)
            pe.wait_ge(bent, 1)
            n = 0
            for c in range(4):
                for m in range(3):
                    n += 1
                    if n > 3:
                        pe.wait_ge(taken, n - 3)
                    rows = slice(0, 64) if m < 2 else slice(64, 128)
                    for s, (t0, w) in enumerate(RW_SPANS):
                        mm = pe.matmul(ps[:, 2 * (n % 3) + s, 0:w], w2[rows, m, c * P:(c + 1) * P],
                                       f[rows, RW_WA, 1 + t0:1 + t0 + w], start=True, stop=True)
                    mm.then_inc(summed, 1)
            for c in range(4):
                pe.wait_ge(bent, c + 2)
                if c >= 1:
                    pe.wait_ge(rooted, c)
                for s, (t0, w) in enumerate(RW_SPANS):
                    mm = pe.matmul(ps[:, 6 + s, 0:w], kit.const("head_ones"), tmp[2 + c % 2][:, t0:t0 + w],
                                   start=True, stop=True)
                mm.then_inc(ksummed, 1)


HALVES = (slice(0, 64), slice(64, 128))


def rwkv_scan(kit, f, cum, kk, b_neg, y_out, spare, decays, bearer):
    nc, ph, ps = kit.nc, kit.ph, kit.ps
    big, small = 512, 256
    class Dir:
        pass

    dirs = []
    for d in range(2):
        t = Dir()
        bigs = kit.ring[:, 0:12 * big] if d == 0 else spare
        smalls = (kit.ring[:, 12 * big:12 * big + 6 * small] if d == 0
                  else kit.ring[:, 12 * big + 6 * small:12 * big + 12 * small])
        names = ["kk_bd", "k_bd", "b_bd", "kk_tm", "k_tm", "b_tm", "n_t", "auk_t", "x", "z", "v_bd", "s_bd"]
        t.big = {n: bigs[:, j * big:(j + 1) * big].rearrange("p (q n) -> p q n", q=4) for j, n in enumerate(names)}
        t.big["yl"], t.big["w_t"] = t.big["b_bd"], t.big["kk_bd"]
        t.big["g0"], t.big["u"] = t.big["n_t"], t.big["auk_t"]
        names = ["r", "rk", "rb", "chunk_cum", "grow", "v_chunk"]
        t.small = {n: smalls[:, j * small:(j + 1) * small].rearrange("p (q n) -> p q n", q=4)
                   for j, n in enumerate(names)}
        t.decay = decays[:, d]
        t.fwd = d == 0
        t.own = t.decay[:, :, 1:65] if t.fwd else t.decay[:, :, 0:64]
        t.before = t.decay[:, :, 0:64] if t.fwd else t.decay[:, :, 1:65]
        t.end = 64 if t.fwd else 0
        t.strict = "s_lt_t" if t.fwd else "s_gt_t"
        t.inclusive = "s_le_t" if t.fwd else "s_ge_t"
        t.bearer = bearer[:, d:d + 1]
        t.bank = 4 * d
        t.cum, t.y = cum[d], y_out[d]
        t.merge = [("merge%d" if t.fwd else "mergeT%d") % l for l in range(6)]
        t.mergeT = [("mergeT%d" if t.fwd else "merge%d") % l for l in range(6)]
        dirs.append(t)

    order = [("act", "grown"), ("act", "identity"), ("dve", "bd"), ("pe", "scores"), ("act", "v_copied"),
             ("dve", "masked"), ("dve", "aux"), ("pe", "turned"), ("act", "tm")]
    for l in range(1, 6):
        order += [("pe", f"y{l}"), ("act", f"yl{l}"), ("pe", f"p{l}"), ("dve", f"x{l}")]
    order += [("pe", "wg"), ("act", "w"), ("dve", "g0"), ("pe", "u"), ("act", "u"), ("pe", "out"), ("act", "y"),
              ("dve", "s")]
    pe_names, act_names, dve_names = ([n for e, n in order if e == engine] for engine in ("pe", "act", "dve"))

    for t in dirs:
        t.pe = Steps(ph.sem("scan_pe"), *pe_names)
        t.act = Steps(ph.sem("scan_act"), *act_names)
        t.dve = Steps(ph.sem("scan_dve"), *dve_names)
    lag = 4 * 4
    chunks = (CTX // 64, SEQ // 64)

    def run(engine, fori, step):
        def turn(i, part, leading=True, trailing=True, before=None):
            started = part * chunks[0]
            for k in range(len(order)):
                if leading and order[k][0] == engine:
                    step(dirs[0], i, part, i + started, order[k][1])
                at = k - lag
                if at < 0 and before is not False and order[at][0] == engine:
                    j, p = before or (i - 1, part)
                    step(dirs[1], j, p, j + p * chunks[0], order[at][1])
                if at >= 0 and trailing and order[at][0] == engine:
                    step(dirs[1], i, part, i + started, order[at][1])

        turn(0, 0, before=False)
        with fori(1, chunks[0]) as i:
            turn(i, 0)
        turn(0, 1, before=(chunks[0] - 1, 0))
        with fori(1, chunks[1]) as i:
            turn(i, 1)
        turn(0, 1, leading=False, trailing=False, before=(chunks[1] - 1, 1))

    zeroed = [ph.sem("scan_zeroed") for _ in dirs]
    for t in dirs:
        t.mid = ph.sem("scan_mid")

    def bank(t, k):
        return ps[:, t.bank + k, :].rearrange("p (q n) -> p q n", q=4)

    def offset(t, part, i):
        n, at = (CTX // 64, 0) if part == 0 else (SEQ // 64, CTX + 1)
        return i * 64 + at if t.fwd else i * -64 + (at + 64 * (n - 1))

    with ph as block:
        @block.tensor
        def _(pe):
            def step(t, turn, name):
                m = t.big
                wait = lambda s, n: pe.wait_ge(s.done, s.value(turn, n))
                if name == "scores":
                    wait(t.dve, "bd")
                    wait(t.act, "grown")
                    for k, (lhs, rhs) in enumerate((("b_bd", "kk_bd"), ("kk_bd", "b_bd"), ("k_bd", "kk_bd"))):
                        for q in range(4):
                            pe.matmul(bank(t, k)[:, q, :], m[lhs][:, q, :], m[rhs][:, q, :], start=True, stop=True)
                    half = ps[:, t.bank + 3, :].rearrange("p (m q n) -> p m q n", m=2, q=4)
                    for k, lhs in enumerate(("k_bd", "b_bd")):
                        for q in range(4):
                            mm = pe.matmul(half[:, k, q, :], m[lhs][:, q, :], t.small["r"][:, q, :],
                                           start=True, stop=True)
                elif name == "turned":
                    wait(t.dve, "aux")
                    wait(t.act, "v_copied")
                    for k, src in enumerate(("kk_bd", "k_bd", "b_bd")):
                        for q in range(4):
                            pe.transpose(bank(t, k)[:, q, :], m[src][:, q, :], kit.const("ident"))
                    for q in range(4):
                        mm = pe.transpose(ps[0:64, t.bank + 3, q * P:(q + 1) * P], t.small["v_chunk"][:, q, :],
                                          kit.const("ident"))
                elif name[0] == "y":
                    l = int(name[1:])
                    if l == 1:
                        wait(t.act, "tm")
                    else:
                        wait(t.dve, f"x{l - 1}")
                    for q in range(4):
                        mm = pe.matmul(bank(t, 0)[:, q, :], m["n_t"][:, q, :], m["x"][:, q, :], start=True, stop=True)
                elif name[0] == "p":
                    wait(t.act, f"yl{name[1:]}")
                    for q in range(4):
                        pe.matmul(bank(t, 1)[:, q, :], m["z"][:, q, :], m["yl"][:, q, :], start=True, stop=True)
                    for q in range(4):
                        mm = pe.matmul(bank(t, 2)[:, q, :], m["yl"][:, q, :], m["z"][:, q, :], start=True, stop=True)
                elif name == "wg":
                    wait(t.dve, "x5")
                    for q in range(4):
                        pe.matmul(bank(t, 0)[:, q, :], m["kk_tm"][:, q, :], m["z"][:, q, :], start=True, stop=True)
                    for q in range(4):
                        mm = pe.matmul(bank(t, 1)[:, q, :], m["auk_t"][:, q, :], m["v_bd"][:, q, :],
                                       start=True, stop=True)
                elif name == "u":
                    wait(t.act, "w")
                    wait(t.dve, "g0")
                    for q in range(4):
                        pe.matmul(bank(t, 2)[:, q, :], m["z"][:, q, :], m["g0"][:, q, :], start=True, stop=False)
                        mm = pe.matmul(bank(t, 2)[:, q, :], m["w_t"][:, q, :], m["s_bd"][:, q, :],
                                       start=False, stop=True)
                elif name == "out":
                    wait(t.act, "u")
                    for q in range(4):
                        pe.matmul(bank(t, 3)[:, q, :], m["k_tm"][:, q, :], m["v_bd"][:, q, :], start=True, stop=False)
                        pe.matmul(bank(t, 3)[:, q, :], m["b_tm"][:, q, :], m["u"][:, q, :], start=False, stop=True)
                    y = ps[:, t.bank, 0:256].rearrange("p (q n) -> p q n", q=4)
                    for q in range(4):
                        pe.matmul(y[:, q, :], m["s_bd"][:, q, :], t.small["r"][:, q, :], start=True, stop=False)
                        pe.matmul(y[:, q, :], m["v_bd"][:, q, :], t.small["rk"][:, q, :], start=False, stop=False)
                        mm = pe.matmul(y[:, q, :], m["u"][:, q, :], t.small["rb"][:, q, :], start=False, stop=True)
                mm.then_inc(t.pe.done, 1)

            for t in dirs:
                pe.wait_ge(zeroed[dirs.index(t)], 1)
                pe.transpose(ps[:, t.bank, 0:P], kit.const("ident"), kit.const("ident")).then_inc(t.pe.done, 1)
            run("pe", pe.Fori, lambda t, i, part, turn, name: step(t, turn, name))

        @block.scalar
        def _(act):
            def step(t, turn, at, part, name):
                m = t.big
                wait = lambda s, n: act.wait_ge(s.done, s.value(turn, n))
                if name == "grown":
                    act.wait_ge(t.dve.done, t.dve.before(turn))
                    act.wait_ge(t.pe.done, t.pe.before(turn))
                    act.activation(t.own, t.cum[:, :, bass.ds(at, 64)], ACT.Exp)
                    ins = act.activation(t.small["grow"], t.cum[:, :, bass.ds(at, 64)], ACT.Exp, scale=-1.0)
                elif name == "identity":
                    for n in ("x", "z"):
                        ins = act.activation(m[n], over(kit.const("ident"), 4), ACT.Copy)
                elif name == "v_copied":
                    ins = act.activation(t.small["v_chunk"], f[:, RW_V:RW_V + 4, bass.ds(at + 1, 64)], ACT.Copy)
                elif name == "tm":
                    wait(t.pe, "turned")
                    for k, n in enumerate(("kk_tm", "k_tm", "b_tm")):
                        act.activation(m[n], bank(t, k), ACT.Copy)
                    for q, half in enumerate(HALVES):
                        ins = act.activation(m["v_bd"][half, :, half], bank(t, 3)[0:64, :, half], ACT.Copy)
                elif name[:2] == "yl":
                    wait(t.pe, f"y{name[2:]}")
                    ins = act.activation(m["yl"], bank(t, 0), ACT.Copy)
                elif name == "w":
                    wait(t.pe, "wg")
                    ins = act.activation(m["w_t"], bank(t, 0), ACT.Copy)
                elif name == "u":
                    wait(t.pe, "u")
                    ins = act.activation(m["u"], bank(t, 2), ACT.Copy)
                elif name == "y":
                    wait(t.pe, "out")
                    ins = act.activation(t.y(at, part), ps[:, t.bank, 0:256].rearrange("p (q n) -> p q n", q=4), ACT.Copy)
                ins.then_inc(t.act.done, 1)

            for t in dirs:
                one = t.decay[:, :, 0:1] if t.fwd else t.decay[:, :, 64:65]
                act.activation(one, kit.const("ones")[:, 0:4].unsqueeze(2), ACT.Copy).then_inc(t.act.done, 1)
            run("act", act.Fori, lambda t, i, part, turn, name: step(t, turn, offset(t, part, i), part, name))

        @block.vector
        def _(dve):
            def step(t, turn, at, name):
                m = t.big
                wait = lambda s, n: dve.wait_ge(s.done, s.value(turn, n))
                if name == "bd":
                    dve.wait_ge(t.pe.done, t.pe.before(turn))
                    dve.wait_ge(t.act.done, t.act.value(turn, "grown"))
                    for half in HALVES:
                        dve.tensor_tensor(m["kk_bd"][half, :, half], kk[half, :, bass.ds(at, 64)],
                                          t.before[half], ALU.mult)
                        dve.tensor_tensor(m["k_bd"][half, :, half], f[half, RW_K:RW_K + 4, bass.ds(at + 1, 64)],
                                          t.small["grow"][half], ALU.mult)
                        dve.tensor_tensor(m["b_bd"][half, :, half], b_neg[half, :, bass.ds(at, 64)],
                                          t.small["grow"][half], ALU.mult)
                    ins = dve.tensor_tensor(t.small["r"], f[:, RW_R:RW_R + 4, bass.ds(at + 1, 64)], t.own, ALU.mult)
                elif name == "masked":
                    wait(t.pe, "scores")
                    wait(t.act, "identity")
                    dve.tensor_tensor(m["n_t"], bank(t, 0), over(kit.const(t.strict), 4), ALU.mult)
                    dve.copy_predicated(m["x"], over(kit.const(t.merge[0]), 4).bitcast(mybir.dt.uint32), bank(t, 1))
                    ins = dve.copy_predicated(m["z"], over(kit.const(t.mergeT[0]), 4).bitcast(mybir.dt.uint32),
                                              bank(t, 0))
                elif name == "aux":
                    dve.tensor_tensor(m["auk_t"], bank(t, 2), over(kit.const(t.strict), 4), ALU.mult)
                    mask = kit.const(t.inclusive)
                    for k, n in enumerate(("rk", "rb")):
                        half_bank = ps[:, t.bank + 3, k * 256:(k + 1) * 256].rearrange("p (q n) -> p q n", q=4)
                        for half in HALVES:
                            ins = dve.tensor_tensor(
                                t.small[n][half], half_bank[half],
                                mask[half, half].unsqueeze(1).broadcast_to([64, 4, 64]), ALU.mult)
                elif name[0] == "x":
                    l = int(name[1:])
                    wait(t.pe, f"p{l}")
                    dve.tensor_copy(t.bearer, kit.const("ones")[:, 0:1])
                    dve.copy_predicated(m["x"], over(kit.const(t.merge[l]), 4).bitcast(mybir.dt.uint32), bank(t, 1))
                    ins = dve.copy_predicated(m["z"], over(kit.const(t.mergeT[l]), 4).bitcast(mybir.dt.uint32),
                                              bank(t, 2))
                elif name == "g0":
                    wait(t.pe, "wg")
                    ins = dve.tensor_copy(m["g0"], bank(t, 1))
                elif name == "s":
                    wait(t.pe, "out")
                    ends = t.decay[:, :, t.end:t.end + 1]
                    dve.tensor_tensor(m["s_bd"], m["s_bd"], bank(t, 3), ALU.add).then_inc(t.mid, 1)
                    dve.wait_ge(t.mid, turn + 1)
                    ins = dve.tensor_tensor(m["s_bd"], m["s_bd"], ends.broadcast_to([P, 4, P]), ALU.mult)
                ins.then_inc(t.dve.done, 1)

            for d, t in enumerate(dirs):
                for n in ("kk_bd", "k_bd", "b_bd", "v_bd"):
                    dve.memset(t.big[n], 0.0)
                dve.memset(t.big["s_bd"], 0.0).then_inc(zeroed[d], 1)
                dve.wait_ge(zeroed[d], 1)
                dve.memset(t.small["rk"], 0.0).then_inc(t.dve.done, 1)
            run("dve", dve.Fori, lambda t, i, part, turn, name: step(t, turn, offset(t, part, i), name))


def rwkv_finish(kit, f, g2_dram, pack2, y_f, y_b, scratch):
    nc, ph, ps = kit.nc, kit.ph, kit.ps
    ring = kit.ring
    g2 = ring[:, 0:512]
    spans = spans_of(T2)

    def col(name, c):
        at = PACK2_AT[name] + c
        return pack2(slice(at, at + 1))

    def tokens(row, n):
        t0, w = spans[n]
        return row[:, 1 + t0 + n:1 + t0 + n + w]

    loaded, multiplied, ordered, summed, acted = (
        ph.sem(f"fin_{s}") for s in ("loaded", "multiplied", "ordered", "summed", "acted"))
    tmp, sq, stat = scratch
    with ph as block:
        @block.sync
        def _(sp):
            sp.dma_start(g2, g2_dram).then_inc(loaded, 16)
            sp.wait_ge(loaded, 16)

        @block.vector
        def _(dve):
            chain = Chain(dve, ordered)
            for c in range(4):
                chain(dve.tensor_tensor(y_f[:, c, :], y_f[:, c, :], y_b[:, c, :], ALU.add))
                for n, (t0, w) in enumerate(spans):
                    chain(dve.scalar_tensor_tensor(out=tmp[:, c, t0:t0 + w], in0=tokens(f[:, RW_R + c, :], n),
                                                   scalar=col("r_k", c), in1=tokens(f[:, RW_K + c, :], n),
                                                   op0=ALU.mult, op1=ALU.mult))
                dve.sem_inc(multiplied, 1)
                dve.wait_ge(summed, 2 * c + 1)
                for n, (t0, w) in enumerate(spans):
                    chain(dve.scalar_tensor_tensor(out=y_f[:, c, t0:t0 + w], in0=ps[:, n, 0:w], scalar=-1.0 / 64,
                                                   in1=y_f[:, c, t0:t0 + w], op0=ALU.mult, op1=ALU.add))
                    chain(dve.tensor_tensor(tmp[:, c, t0:t0 + w], ps[:, 2 + n, 0:w],
                                            tokens(f[:, RW_V + c, :], n), ALU.mult))
                chain(dve.tensor_tensor(sq[:, c, :], y_f[:, c, :], y_f[:, c, :], ALU.mult))
                dve.sem_inc(multiplied, 1)
                dve.wait_ge(summed, 2 * c + 2)
                for n, (t0, w) in enumerate(spans):
                    chain(dve.tensor_scalar(stat[:, c, t0:t0 + w], ps[:, 4 + n, 0:w], 1.0 / 64, GN_EPS,
                                            ALU.mult, ALU.add))
                dve.sem_inc(multiplied, 1)
                dve.wait_ge(acted, c + 1)
                chain(dve.reciprocal(stat[:, c, :], stat[:, c, :]))
                chain(dve.scalar_tensor_tensor(out=y_f[:, c, :], in0=y_f[:, c, :], scalar=col("lnx_w", c),
                                               in1=stat[:, c, :], op0=ALU.mult, op1=ALU.mult))
                chain(dve.scalar_tensor_tensor(out=y_f[:, c, :], in0=y_f[:, c, :], scalar=col("lnx_b", c),
                                               in1=tmp[:, c, :], op0=ALU.add, op1=ALU.add))
                for n, (t0, w) in enumerate(spans):
                    chain(dve.tensor_tensor(y_f[:, c, t0:t0 + w], y_f[:, c, t0:t0 + w], ps[:, 6 + n, 0:w], ALU.mult))
                dve.sem_inc(multiplied, 1)

        @block.scalar
        def _(act):
            for c in range(4):
                act.wait_ge(multiplied, 4 * c + 3)
                act.activation(stat[:, c, :], stat[:, c, :], ACT.Sqrt).then_inc(acted, 1)

        @block.tensor
        def _(pe):
            pe.wait_ge(loaded, 16)
            for c in range(4):
                pe.wait_ge(multiplied, 4 * c + 1)
                for n, (t0, w) in enumerate(spans):
                    pe.matmul(ps[:, n, 0:w], kit.const("head_ones"), y_f[:, c, t0:t0 + w], start=True, stop=True)
                    mm = pe.matmul(ps[:, 2 + n, 0:w], kit.const("head_ones"), tmp[:, c, t0:t0 + w],
                                   start=True, stop=True)
                mm.then_inc(summed, 1)
                pe.wait_ge(multiplied, 4 * c + 2)
                for n, (t0, w) in enumerate(spans):
                    pe.matmul(ps[:, 4 + n, 0:w], kit.const("head_ones"), sq[:, c, t0:t0 + w], start=True, stop=True)
                    mm = pe.matmul(ps[:, 6 + n, 0:w], g2[:, c * P:(c + 1) * P], tokens(f[:, RW_G, :], n),
                                   start=True, stop=True)
                mm.then_inc(summed, 1)


SSM_Z, SSM_X, SSM_B, SSM_C = 0, 4, 8, 10
SSM_COLS, AT_DT, AT_GLA, AT_GD = 1536, 1536, 1552, 3088


def ssm_branch(kit, h, pack2, w_in, y, gd):
    nc, ph, ps = kit.nc, kit.ph, kit.ps
    ring = kit.ring
    chunks = T2 // P

    def col(name, c):
        at = PACK2_AT[name] + c
        return pack2(slice(at, at + 1))

    def cols(name, n, c=0):
        at = PACK2_AT[name] + c
        return pack2(slice(at, at + n))

    with ExitStack() as ctx:
        def sb(name, shape):
            return ctx.enter_context(nc.sbuf_tensor(name, shape, F32))

        conv, (low_place,) = kit.shared(ctx, "ssm_conv", [P, 8, WS], [("ssm_project_x_lo", [KD, T2])])
        dt = sb("ssm_dt", [P, chunks, 16])
        gate = y[:, 4:8, :]
        with nc.sbuf_tensor("ssm_raw", [P, 12, WS + 4], F32) as raw:
            flat = raw[:, :, :].rearrange("p k n -> p (k n)")
            width = WS + 4

            def store(act, j, banks):
                for n, ((t0, w), bank) in enumerate(zip(spans_of(T2), banks)):
                    ins = act.activation(flat[:, bass.ds(j * width + (2 + t0 + 2 * n), w)], bank, ACT.Copy)
                return ins

            gemm(kit, "ssm_project", w_in[:, :, 0:SSM_COLS], SSM_COLS, h, T2, store,
                 low_place=low_place)

            w_small = ring[:, 0:KD * 32].rearrange("p (k n) -> p k n", k=KD)
            sums = ring[:, 256:256 + 16 * chunks].rearrange("p (c n) -> p c n", n=16)
            tmps = ring[:, 1024:1024 + 2 * WS].rearrange("p (u n) -> p u n", u=2)
            rate = ring[:, 512:528]
            loaded, summed, stepped, acted, padded, tapped, bent, gated = (
                ph.sem(f"ssm_{s}") for s in
                ("loaded", "summed", "stepped", "acted", "padded", "tapped", "bent", "gated"))
            act_steps = ph.sem("ssm_act_steps")
            with ph as block:
                @block.sync
                def _(sp):
                    sp.dma_start(w_small[:, :, 0:16], w_in[:, :, AT_DT:AT_GLA]).then_inc(loaded, 16)
                    sp.dma_start(w_small[:, :, 16:32], w_in[:, :, AT_GD:AT_GD + 16]).then_inc(loaded, 16)
                    sp.wait_ge(loaded, 32)

                @block.tensor
                def _(pe):
                    pe.wait_ge(loaded, 32)
                    for c in range(chunks):
                        for k in range(KD):
                            mm = pe.matmul(ps[:, 0, c * 16:(c + 1) * 16], h[:, k, c * P:(c + 1) * P],
                                           w_small[:, k, 0:16], start=(k == 0), stop=(k == KD - 1))
                    mm.then_inc(summed, 1)
                    for n, (t0, w) in enumerate(spans_of(T2)):
                        for k in range(KD):
                            mm = pe.matmul(ps[0:16, 1 + n, 0:w], w_small[:, k, 16:32], h[:, k, t0:t0 + w],
                                           start=(k == 0), stop=(k == KD - 1))
                    mm.then_inc(summed, 1)

                @block.gpsimd
                def _(pool):
                    for at in (0, 2 + CTX, width - 2):
                        ins = pool.memset(raw[:, :, at:at + 2], 0.0)
                    ins.then_inc(padded, 1)

                @block.vector
                def _(dve):
                    chain = Chain(dve, stepped)
                    dve.wait_ge(summed, 1)
                    logits = ps[:, 0, 0:16 * chunks].rearrange("p (c n) -> p c n", n=16)
                    chain(dve.tensor_tensor(sums, logits, over(cols("dt_bias", 16), chunks), ALU.add))
                    dve.wait_ge(acted, 1)
                    chain(dve.scalar_tensor_tensor(out=dt[:, :, :], in0=sums, scalar=0.0, in1=dt[:, :, :],
                                                   op0=ALU.max, op1=ALU.add))
                    dve.wait_ge(padded, 1)
                    for n in range(5):
                        for c in range(8):
                            src = raw[:, SSM_X + c, n:n + WS]
                            tap = col("conv_w", c * 5 + n)
                            if n == 0:
                                op = dve.tensor_scalar(conv[:, c, :], src, tap, col("conv_b", c), ALU.mult, ALU.add)
                            else:
                                dve.wait_ge(tapped, 8 * (n - 1) + c + 1)
                                op = dve.scalar_tensor_tensor(out=conv[:, c, :], in0=src, scalar=tap,
                                                              in1=conv[:, c, :], op0=ALU.mult, op1=ALU.add)
                            op.then_inc(tapped, 1)
                    for c in range(8):
                        dve.wait_ge(bent, c + 1)
                        dve.tensor_tensor(conv[:, c, :], conv[:, c, :], tmps[:, c % 2, :], ALU.mult).then_inc(gated, 1)
                    for c in range(4):
                        dve.wait_ge(bent, 9 + c)
                        dve.tensor_tensor(gate[:, c, :], gate[:, c, :], raw[:, SSM_Z + c, width - 2 - SEQ:width - 2],
                                          ALU.mult)

                @block.scalar
                def _(act):
                    chain = Chain(act, act_steps)
                    act.wait_ge(stepped, 1)
                    chain(act.activation(dt[:, :, :], sums, ACT.Abs))
                    chain(act.activation(dt[:, :, :], dt[:, :, :], ACT.Exp, scale=-1.0))
                    act.activation(dt[:, :, :], dt[:, :, :], ACT.Ln, bias=1.0).then_inc(acted, 1)
                    act.activation(rate, cols("a_log", 16), ACT.Exp)
                    act.wait_ge(summed, 2)
                    for n, (t0, w) in enumerate(spans_of(T2)):
                        act.activation(gd[0:16, t0:t0 + w], ps[0:16, 1 + n, 0:w], ACT.Copy)
                    for c in range(8):
                        act.wait_ge(tapped, 32 + c + 1)
                        if c >= 2:
                            act.wait_ge(gated, c - 1)
                        act.activation(tmps[:, c % 2, :], conv[:, c, :], ACT.Sigmoid).then_inc(bent, 1)
                    for c in range(4):
                        act.activation(gate[:, c, :], raw[:, SSM_Z + c, width - 2 - SEQ:width - 2],
                                       ACT.Sigmoid).then_inc(bent, 1)
        y_tok = sb("ssm_y", [P, SEQ // P, 512])
        state = sb("ssm_state", [P, 2, 512])
        la = sb("ssm_log_decay", [P, chunks, 16])
        work = ExitStack()
        with work:
            def wb(name, shape):
                return work.enter_context(nc.sbuf_tensor(name, shape, F32))

            la_wide = wb("la_wide", [P, 2, 8, P])
            lmat = wb("lmat", [P, 2, 8, P])
            b_tok = wb("b_tok", [P, 2, P])
            cb = wb("cb", [P, 2, 2, P])
            xdt, xw = wb("xdt", [P, 2, 512]), wb("xw", [P, 2, 512])
            cum, grown, end_decay, w_end = (wb(n, [P, 2, 8]) for n in ("ssm_cum", "ssm_grown", "ssm_ends", "ssm_w"))
            inter = wb("inter", [P, 2, 512])
            sl, dd, aa, mm_done = (ph.sem(f"ssd_{s}") for s in ("rated", "dve", "act", "pe"))
            n_ctx = CTX // P
            order = (list(range(chunks)), list(range(n_ctx))[::-1] + list(range(n_ctx, chunks))[::-1])

            def column(c):
                return c * P + (2 if c >= n_ctx else 0)

            with ph as block:
                steps = [(i, d) for i in range(chunks) for d in range(2)]
                PE_N, DVE_N, ACT_N = 3, 6, 3

                @block.tensor
                def _(pe):
                    for u, (i, d) in enumerate(steps):
                        c = order[d][i]
                        at = column(c)
                        mask = kit.const("j_le_i" if d == 0 else "j_ge_i")
                        latent = c >= n_ctx
                        if u >= 1:
                            pe.wait_ge(dd, 1 + DVE_N * u)
                            pe.wait_ge(aa, 1 + ACT_N * u)
                        for q in range(4):
                            pe.transpose(ps[:, 0, q * P:(q + 1) * P], conv[:, q, at:at + P], kit.const("ident"))
                        for g in range(2):
                            pe.transpose(ps[:, 1, g * P:(g + 1) * P], conv[:, 4 + g, at:at + P], kit.const("ident"))
                        for g in range(2):
                            mm = pe.matmul(ps[:, 1, (2 + g) * P:(3 + g) * P], conv[:, 4 + g, at:at + P],
                                           conv[:, 6 + g, at:at + P], start=True, stop=True)
                        mm.then_inc(mm_done, 1)
                        pe.wait_ge(dd, 1 + DVE_N * u + 1)
                        pe.matmul(ps[:, 2, 0:8], mask, la[:, c, 8 * d:8 * d + 8], start=True, stop=True)
                        for hd in range(8):
                            mm = pe.matmul(ps[:, 3 + hd // 4, (hd % 4) * P:(hd % 4 + 1) * P], la_wide[:, d, hd, :], mask,
                                           start=True, stop=True)
                        mm.then_inc(mm_done, 1)
                        pe.wait_ge(dd, 1 + DVE_N * u + 5)
                        if latent:
                            for hd in range(8):
                                pe.matmul(ps[:, 5, hd * 64:(hd + 1) * 64], lmat[:, d, hd, :],
                                          xdt[:, d, hd * 64:(hd + 1) * 64], start=True, stop=True)
                            for g in range(2):
                                pe.matmul(ps[:, 6, g * 256:(g + 1) * 256], conv[:, 6 + g, at:at + P],
                                          state[:, d, g * 256:(g + 1) * 256], start=True, stop=True)
                        for g in range(2):
                            mm = pe.matmul(ps[:, 7, g * 256:(g + 1) * 256], b_tok[:, g, :],
                                           xw[:, d, g * 256:(g + 1) * 256], start=True, stop=True)
                        mm.then_inc(mm_done, 1)

                @block.scalar
                def _(act):
                    act.activation(end_decay[:, 0, :], kit.const("ones")[:, 0:8], ACT.Copy).then_inc(aa, 1)
                    for u, (i, d) in enumerate(steps):
                        c = order[d][i]
                        act.wait_ge(mm_done, PE_N * u + 1)
                        act.activation(b_tok[:, :, :].rearrange("p g n -> p (g n)"), ps[:, 1, 0:256],
                                       ACT.Copy).then_inc(aa, 1)
                        act.wait_ge(dd, 1 + DVE_N * u + 2)
                        act.activation(grown[:, d, :], cum[:, d, :], ACT.Exp)
                        act.activation(w_end[:, d, :], w_end[:, d, :], ACT.Exp)
                        act.activation(end_decay[:, d, :], end_decay[:, d, :], ACT.Exp).then_inc(aa, 1)
                        act.wait_ge(dd, 1 + DVE_N * u + 3)
                        act.activation(lmat[:, d, :, :], lmat[:, d, :, :], ACT.Exp).then_inc(aa, 1)

                @block.vector
                def _(dve):
                    chain = Chain(dve, sl)
                    chain(dve.scalar_tensor_tensor(out=la[:, :, :], in0=dt[:, :, :], scalar=-1.0,
                                                   in1=over(rate, chunks), op0=ALU.mult, op1=ALU.mult))
                    dve.memset(state[:, :, :], 0.0).then_inc(dd, 1)
                    for u, (i, d) in enumerate(steps):
                        c = order[d][i]
                        latent = c >= n_ctx
                        last = P - 1 if d == 0 else 0
                        if u >= 1:
                            dve.wait_ge(mm_done, PE_N * u)
                        dve.tensor_copy(la_wide[:, d, :, :], along(la[:, c, 8 * d:8 * d + 8], P)).then_inc(dd, 1)
                        dve.wait_ge(mm_done, PE_N * u + 2)
                        dve.wait_ge(aa, 1 + ACT_N * u)
                        spread = ps[:, 3:5, :].rearrange("p b (h n) -> p (b h) n", n=P)
                        chain(dve.tensor_copy(cum[:, d, :], ps[:, 2, 0:8]))
                        chain(dve.tensor_copy(end_decay[:, d, :], spread[:, :, last:last + 1].rearrange("p h n -> p (h n)")))
                        dve.tensor_tensor(w_end[:, d, :], end_decay[:, d, :], cum[:, d, :], ALU.subtract).then_inc(dd, 1)
                        for hd in range(8):
                            ins = dve.tensor_scalar(lmat[:, d, hd, :], spread[:, hd, :], cum[:, d, hd:hd + 1], 0.0,
                                                    ALU.subtract, ALU.min)
                        ins.then_inc(dd, 1)
                        dve.wait_ge(aa, 1 + ACT_N * u + 2)
                        chain(dve.tensor_tensor(xdt[:, d, :].rearrange("p (h n) -> p h n", h=8),
                                                ps[:, 0, :].rearrange("p (h n) -> p h n", h=8),
                                                along(dt[:, c, 8 * d:8 * d + 8], 64), ALU.mult))
                        chain(dve.tensor_tensor(cb[:, d, :, :], ps[:, 1, 256:512].rearrange("p (g n) -> p g n", g=2),
                                                over(kit.const("j_le_i" if d == 0 else "j_ge_i"), 2), ALU.mult))
                        dve.tensor_tensor(xw[:, d, :].rearrange("p (h n) -> p h n", h=8),
                                          xdt[:, d, :].rearrange("p (h n) -> p h n", h=8),
                                          along(w_end[:, d, :], 64), ALU.mult).then_inc(dd, 1)
                        dve.wait_ge(aa, 1 + ACT_N * u + 3)
                        for g in range(2):
                            ins = dve.tensor_tensor(lmat[:, d, 4 * g:4 * g + 4, :], lmat[:, d, 4 * g:4 * g + 4, :],
                                                    over(cb[:, d, g, :], 4), ALU.mult)
                        ins.then_inc(dd, 1)
                        dve.wait_ge(mm_done, PE_N * u + 3)
                        if latent:
                            out = y_tok[:, c - n_ctx, :]
                            t = inter[:, d, :]
                            chain(dve.tensor_tensor(t.rearrange("p (h n) -> p h n", h=8),
                                                    ps[:, 6, :].rearrange("p (h n) -> p h n", h=8),
                                                    along(grown[:, d, :], 64), ALU.mult))
                            if not first_write(order, c, i, d):
                                chain(dve.tensor_tensor(out, out, t, ALU.add))
                                t = out
                            chain(dve.tensor_tensor(out, t, ps[:, 5, :], ALU.add))
                        s = state[:, d, :].rearrange("p (h n) -> p h n", h=8)
                        chain(dve.tensor_tensor(s, s, along(end_decay[:, d, :], 64), ALU.mult))
                        dve.tensor_tensor(state[:, d, :], state[:, d, :], ps[:, 7, :], ALU.add).then_inc(dd, 1)

        to_channels(kit, "ssm_y", y_tok, SEQ // P, y)
        scratch = ring[:, 0:4 * SEQ].rearrange("p (c n) -> p c n", c=4)
        skipped = ph.sem("ssm_skipped")
        stepped = ph.sem("ssm_ordered")
        with ph as block:
            @block.vector
            def _(dve):
                chain = Chain(dve, stepped)
                for c in range(4):
                    chain(dve.scalar_tensor_tensor(out=y[:, c, 0:SEQ], in0=conv[:, c, CTX + 2:], scalar=col("d_skip", c),
                                                   in1=y[:, c, 0:SEQ], op0=ALU.mult, op1=ALU.add))
                    dve.tensor_tensor(y[:, c, 0:SEQ], y[:, c, 0:SEQ], gate[:, c, :], ALU.mult).then_inc(skipped, 1)
        for g in range(2):
            part = y[:, 2 * g:2 * g + 2, 0:SEQ]
            norm(kit, "ssm_group", part, 2, SEQ, lambda j, n, g=g: col("ssm_norm", 2 * g + j), part,
                 ring[:, 3 * SEQ:4 * SEQ], squares=scratch)


def first_write(order, c, i, d):
    other = order[1 - d].index(c)
    return i < other or (i == other and d == 0)


GLA_Q, GLA_K, GLA_V, GLA_G = 0, 2, 4, 8
CLIP = 80.0


def gla_branch(kit, h, gd, pack2, w_in, gk_up, y):
    nc, ph, ps = kit.nc, kit.ph, kit.ps
    ring = kit.ring

    def cols(name, n, c=0):
        at = PACK2_AT[name] + c
        return pack2(slice(at, at + n))

    with ExitStack() as ctx:
        def sb(name, shape):
            return ctx.enter_context(nc.sbuf_tensor(name, shape, F32))

        proj = sb("gla_proj", [P, 12, T2])
        flat = proj[:, :, :].rearrange("p k n -> p (k n)")

        def store(act, j, banks):
            for (t0, w), bank in zip(spans_of(T2), banks):
                ins = act.activation(flat[:, bass.ds(j * T2 + t0, w)], bank, ACT.Copy)
            return ins

        gemm(kit, "gla_project", w_in[:, :, AT_GLA:AT_GD], 1536, h, T2, store)
        cum = [sb(f"gla_cum{d}", [P, 2, T2]) for d in range(2)]
        y_back = sb("gla_y_back", [P, 4, SEQ])
        bearer = sb("gla_bearer", [P, 4])

        up = ring[0:16, 0:512].rearrange("p (d n) -> p d n", d=2)
        soft = ring[:, 512:512 + 4 * T2].rearrange("p (m n) -> p m n", m=4)
        resets = ring[:, 512 + 4 * T2:512 + 5 * T2]
        tmp = ring[:, 512 + 5 * T2:512 + 6 * T2]
        loaded, summed, taken, softened, stepped, acts = (
            ph.sem(f"gla_{s}") for s in ("loaded", "summed", "taken", "softened", "stepped", "acts"))
        with ph as block:
            @block.sync
            def _(sp):
                for d in range(2):
                    sp.dma_start(up[:, d, :], gk_up[d]).then_inc(loaded, 16)
                sp.wait_ge(loaded, 32)

            @block.tensor
            def _(pe):
                pe.wait_ge(loaded, 32)
                for m in range(4):
                    for n, (t0, w) in enumerate(spans_of(T2)):
                        mm = pe.matmul(ps[:, 2 * m + n, 0:w], up[:, m // 2, (m % 2) * P:(m % 2 + 1) * P],
                                       gd[0:16, t0:t0 + w], start=True, stop=True)
                    mm.then_inc(summed, 1)

            @block.scalar
            def _(act):
                chain = Chain(act, acts)
                for m in range(4):
                    act.wait_ge(summed, m + 1)
                    for n, (t0, w) in enumerate(spans_of(T2)):
                        ins = act.activation(cum[m // 2][:, m % 2, t0:t0 + w], ps[:, 2 * m + n, 0:w], ACT.Identity,
                                             bias=cols("gk_b", 1, m))
                    chain(ins)
                    chain(act.activation(soft[:, m, :], cum[m // 2][:, m % 2, :], ACT.Abs))
                    chain(act.activation(soft[:, m, :], soft[:, m, :], ACT.Exp, scale=-1.0))
                    act.activation(soft[:, m, :], soft[:, m, :], ACT.Ln, bias=1.0).then_inc(softened, 1)

            @block.vector
            def _(dve):
                chain = Chain(dve, stepped)
                chain(dve.memset(resets, 1.0))
                chain(dve.memset(resets.rearrange("p (n t) -> p n t", t=64)[:, :, 0:1], 0.0))
                for m in range(4):
                    own = cum[m // 2][:, m % 2, :]
                    dve.wait_ge(softened, m + 1)
                    chain(dve.scalar_tensor_tensor(out=own, in0=own, scalar=0.0, in1=soft[:, m, :],
                                                   op0=ALU.min, op1=ALU.subtract))
                    chain(dve.tensor_scalar(own, own, 1.0 / 16, None, ALU.mult))
                    if m < 2:
                        chain(dve.tensor_tensor_scan(own, resets, own, 0.0, ALU.mult, ALU.add))
                    else:
                        chain(dve.tensor_tensor_scan(tmp, resets, own, 0.0, ALU.mult, ALU.add))
                        chain(dve.tensor_tensor(own, own, tmp, ALU.subtract))
                        part = own.rearrange("p (n t) -> p n t", t=64)
                        total = tmp.rearrange("p (n t) -> p n t", t=64)[:, :, 63:64]
                        chain(dve.tensor_tensor(part, part, total.broadcast_to([P, T2 // 64, 64]), ALU.add))

        class Dir:
            pass

        dirs = []
        used = 0

        def take(n):
            nonlocal used
            used += n
            return ring[:, used - n:used]

        for d in range(2):
            t = Dir()
            t.fwd = d == 0
            t.big = {n: take(256).rearrange("p (q n) -> p q n", q=2)
                     for n in ("ka", "qa", "qe", "ke", "ke_tm", "att", "state")}
            t.exps = take(4 * 128).rearrange("p (m q n) -> p m q n", m=4, q=2)
            t.args = take(2 * 128).rearrange("p (m q n) -> p m q n", m=2, q=2)
            t.v_chunk, t.v_tok = take(256).rearrange("p (q n) -> p q n", q=4), take(256).rearrange("p (q n) -> p q n", q=2)
            t.mask = "s_le_t" if t.fwd else "s_ge_t"
            t.cum = cum[d]
            t.bearer, t.first = bearer[:, d:d + 1], bearer[:, 2 + d:3 + d]
            t.bank = 4 * d
            t.middle, t.end = (31, 63) if t.fwd else (32, 0)
            t.pe = Steps(ph.sem("gla_pe"), "att", "turned", "out")
            t.act = Steps(ph.sem("gla_act"), "whole", "v_copied", "grown", "tok")
            t.y_taken = ph.sem("gla_y_taken")
            t.dve = Steps(ph.sem("gla_dve"), "args", "bd", "masked", "state")
            t.mid = ph.sem("gla_mid")
            t.zeroed = ph.sem("gla_zeroed")
            dirs.append(t)
        outs = (y[:, 4:8, :], y_back[:, :, :])

        def offset(t, part, i):
            n, at = (CTX // 64, 0) if part == 0 else (SEQ // 64, CTX)
            return i * 64 + at if t.fwd else i * -64 + (at + 64 * (n - 1))

        def bank(t, k):
            return ps[:, t.bank + k, 0:256].rearrange("p (q n) -> p q n", q=2)

        parts = ((0, CTX // 64), (1, SEQ // 64))
        with ph as block:
            @block.tensor
            def _(pe):
                def step(t, turn, i, part, name):
                    m = t.big
                    if name == "att":
                        if part == 1:
                            pe.wait_ge(t.y_taken, i + 1)
                        pe.wait_ge(t.act.done, t.act.before(turn))
                        pe.wait_ge(t.dve.done, t.dve.value(turn, "bd"))
                        for q in range(2):
                            mm = pe.matmul(bank(t, 0)[:, q, :], m["ka"][:, q, :], m["qa"][:, q, :],
                                           start=True, stop=True)
                    elif name == "turned":
                        pe.wait_ge(t.act.done, t.act.value(turn, "v_copied"))
                        for q in range(2):
                            pe.transpose(bank(t, 1)[:, q, :], m["ke"][:, q, :], kit.const("ident"))
                        for q in range(4):
                            mm = pe.transpose(ps[0:64, t.bank + 2, q * P:(q + 1) * P], t.v_chunk[:, q, :],
                                              kit.const("ident"))
                    else:
                        pe.wait_ge(t.act.done, t.act.value(turn, "tok"))
                        pe.wait_ge(t.dve.done, t.dve.value(turn, "masked"))
                        for q in range(2):
                            mm = pe.matmul(bank(t, 3)[:, q, :], m["ke_tm"][:, q, :], t.v_tok[:, q, :],
                                           start=True, stop=True)
                        if part == 1:
                            for q in range(2):
                                pe.matmul(bank(t, 0)[:, q, :], t.v_tok[:, q, :], m["att"][:, q, :],
                                          start=True, stop=False)
                                mm = pe.matmul(bank(t, 0)[:, q, :], m["state"][:, q, :], m["qe"][:, q, :],
                                               start=False, stop=True)
                    mm.then_inc(t.pe.done, 1)

                for t in dirs:
                    pe.wait_ge(t.zeroed, 1)
                    pe.transpose(ps[:, t.bank, 0:P], kit.const("ident"), kit.const("ident")).then_inc(t.pe.done, 1)
                for part, n in parts:
                    with pe.Fori(0, n) as i:
                        turn = i + part * (CTX // 64)
                        for name in t.pe.names:
                            for t in dirs:
                                step(t, turn, i, part, name)

            @block.scalar
            def _(act):
                def step(t, turn, at, part, name):
                    m = t.big
                    if name == "whole":
                        act.wait_ge(t.pe.done, t.pe.before(turn))
                        act.wait_ge(t.dve.done, t.dve.before(turn))
                        ins = act.activation(t.exps[:, 2], t.cum[:, :, bass.ds(at, 64)], ACT.Exp)
                    elif name == "v_copied":
                        ins = act.activation(t.v_chunk, proj[:, GLA_V:GLA_V + 4, bass.ds(at, 64)], ACT.Copy)
                    elif name == "grown":
                        act.wait_ge(t.dve.done, t.dve.value(turn, "args"))
                        act.activation(t.exps[:, 0], t.args[:, 0], ACT.Exp)
                        act.activation(t.exps[:, 1], t.args[:, 0], ACT.Exp, scale=-1.0)
                        ins = act.activation(t.exps[:, 3], t.args[:, 1], ACT.Exp)
                    elif name == "tok":
                        act.wait_ge(t.pe.done, t.pe.value(turn, "turned"))
                        act.activation(m["ke_tm"], bank(t, 1), ACT.Copy)
                        pairs = ps[0:64, t.bank + 2, :].rearrange("p (q e n) -> p q e n", q=2, e=2)
                        for e, half in enumerate(HALVES):
                            ins = act.activation(t.v_tok[half, :, :], pairs[:, :, e, :], ACT.Copy)
                    else:
                        act.wait_ge(t.pe.done, t.pe.value(turn, "out"))
                        out = outs[dirs.index(t)][:, :, bass.ds(at - CTX, 64)]
                        act.activation(out, ps[:, t.bank, 0:256].rearrange("p (q n) -> p q n", q=4),
                                       ACT.Copy).then_inc(t.y_taken, 1)
                        return
                    ins.then_inc(t.act.done, 1)

                for t in dirs:
                    act.activation(t.exps[:, 0], kit.const("ones").rearrange("p (q n) -> p q n", q=2),
                                   ACT.Copy).then_inc(t.act.done, 1)
                    act.activation(t.first, kit.const("ones")[:, 0:1], ACT.Copy).then_inc(t.y_taken, 1)
                for part, n in parts:
                    with act.Fori(0, n) as i:
                        turn = i + part * (CTX // 64)
                        for name in t.act.names + (("y",) if part == 1 else ()):
                            for t in dirs:
                                step(t, turn, offset(t, part, i), part, name)

            @block.vector
            def _(dve):
                def step(t, turn, at, name):
                    m = t.big
                    if name == "args":
                        dve.wait_ge(t.act.done, t.act.before(turn))
                        c = t.cum[:, :, bass.ds(at, 64)]
                        middle = t.cum[:, :, bass.ds(at + t.middle, 1)].broadcast_to([P, 2, 64])
                        end = t.cum[:, :, bass.ds(at + t.end, 1)].broadcast_to([P, 2, 64])
                        dve.tensor_tensor(t.args[:, 0], c, middle, ALU.subtract).then_inc(t.mid, 1)
                        dve.tensor_tensor(t.args[:, 1], end, c, ALU.subtract)
                        dve.wait_ge(t.mid, turn * 2 + 1)
                        ins = dve.tensor_scalar(t.args[:, 0], t.args[:, 0], CLIP, -CLIP, ALU.min, ALU.max)
                    elif name == "bd":
                        dve.wait_ge(t.pe.done, t.pe.before(turn))
                        dve.wait_ge(t.act.done, t.act.value(turn, "grown"))
                        for n, src, e in (("qa", GLA_Q, 0), ("ka", GLA_K, 1), ("qe", GLA_Q, 2), ("ke", GLA_K, 3)):
                            for half in HALVES:
                                x = proj[half, src:src + 2, bass.ds(at, 64)]
                                out = m[n][half, :, half]
                                ins = dve.tensor_tensor(out, x, t.exps[half, e], ALU.mult)
                    elif name == "masked":
                        dve.wait_ge(t.pe.done, t.pe.value(turn, "att"))
                        dve.tensor_copy(t.bearer, kit.const("ones")[:, 0:1])
                        ins = dve.copy_predicated(m["att"], over(kit.const(t.mask), 2).bitcast(mybir.dt.uint32),
                                                  bank(t, 0))
                    else:
                        dve.wait_ge(t.pe.done, t.pe.value(turn, "out"))
                        end = 63 if t.fwd else 0
                        ends = t.exps[:, 2, :, end:end + 1].broadcast_to([P, 2, P])
                        dve.tensor_tensor(m["state"], m["state"], ends, ALU.mult).then_inc(t.mid, 1)
                        dve.wait_ge(t.mid, turn * 2 + 2)
                        ins = dve.tensor_tensor(m["state"], m["state"], bank(t, 3), ALU.add)
                    ins.then_inc(t.dve.done, 1)

                for t in dirs:
                    for n in ("qa", "ka", "qe", "ke"):
                        dve.memset(t.big[n], 0.0)
                    dve.memset(t.big["state"], 0.0).then_inc(t.zeroed, 1)
                    dve.memset(t.big["att"], 0.0).then_inc(t.dve.done, 1)
                for part, n in parts:
                    with dve.Fori(0, n) as i:
                        turn = i + part * (CTX // 64)
                        for name in t.dve.names:
                            for t in dirs:
                                step(t, turn, offset(t, part, i), name)

        half = ring[:, 0:4 * SEQ].rearrange("p (c n) -> p c n", c=4)
        stepped, bent = ph.sem("gla_added"), ph.sem("gla_bent")
        with ph as block:
            @block.vector
            def _(dve):
                chain = Chain(dve, stepped)
                for c in range(4):
                    chain(dve.tensor_tensor(y[:, 4 + c, 0:SEQ], y[:, 4 + c, 0:SEQ], y_back[:, c, :], ALU.add))
                    dve.tensor_scalar(y[:, 4 + c, 0:SEQ], y[:, 4 + c, 0:SEQ], 0.125, None, ALU.mult)
                for c in range(4):
                    dve.wait_ge(bent, c + 1)
                    dve.tensor_tensor(proj[:, GLA_G + c, CTX:], proj[:, GLA_G + c, CTX:], half[:, c, :], ALU.mult)

            @block.scalar
            def _(act):
                for c in range(4):
                    act.activation(half[:, c, :], proj[:, GLA_G + c, CTX:], ACT.Sigmoid).then_inc(bent, 1)

        for c in range(4):
            part = y[:, 4 + c:5 + c, 0:SEQ]
            norm(kit, "gla_head", part, 1, SEQ, lambda j, n: cols("gla_norm", 1), part, ring[:, 0:SEQ],
                 squares=ring[:, SEQ:2 * SEQ].unsqueeze(1))
        with ph as block:
            @block.vector
            def _(dve):
                for c in range(4):
                    dve.tensor_tensor(y[:, 4 + c, 0:SEQ], y[:, 4 + c, 0:SEQ], proj[:, GLA_G + c, CTX:], ALU.mult)


def conditioning(kit, ctx, x2, d):
    nc, ph = kit.nc, kit.ph

    def sb(name, shape):
        return ctx.enter_context(nc.sbuf_tensor(name, shape, F32))

    pack_sb = sb("pack2", [P, PACK2_WIDTH])
    cvec, mods = sb("cvec", [P, KD, 2]), [sb(f"mods{layer}", [P, 48, 2]) for layer in range(2)]
    sig = sb("c_sigmoid", [P, 16])
    loaded, bent = ph.sem("pack2_loaded"), ph.sem("c_bent")

    def cols(name, n, c=0):
        at = PACK2_AT[name] + c
        return pack_sb[:, at:at + n]

    with ph as block:
        @block.sync
        def _(sp):
            sp.dma_start(pack_sb[:, :], d["pack2"]).then_inc(loaded, 16)
            sp.dma_start(x2[:, :, 0:CTX], d["ctx"]).then_inc(loaded, 16)
            sp.wait_ge(loaded, 32)

        @block.scalar
        def _(act):
            act.wait_ge(loaded, 32)
            act.activation(sig[:, :], cols("c", 16), ACT.Sigmoid).then_inc(bent, 1)

        @block.vector
        def _(dve):
            dve.wait_ge(bent, 1)
            dve.tensor_tensor(cvec[:, :, :].rearrange("p k n -> p (k n)"), cols("c", 16), sig[:, :], ALU.mult)
    return pack_sb, cols, cvec, mods


def second_block(kit, x2, d, pack_sb, cols, mods_of):
    nc, ph = kit.nc, kit.ph
    x_saved = nc.dram_tensor("x_saved", (P, KD, T2), F32, kind="Internal").ap()
    with ExitStack() as ctx:
        def sb(name, shape):
            return ctx.enter_context(nc.sbuf_tensor(name, shape, F32))

        gains = sb("gains", [P, 2, KD, 2])
        h_flat, (h_in_place,) = kit.shared(ctx, "normed2", [P, 8 * W], [("normed2_hi", [KD, T2])])
        h = h_flat[:, 0:KD * T2].rearrange("p (k n) -> p k n", k=KD)
        mods = mods_of[0]

        def pack2(columns):
            return pack_sb[:, columns]

        x_lat = x2[:, :, CTX:]
        norm(kit, "first_norm", x_lat, KD, SEQ, lambda j, n: cols("g_final", 1, j), x_lat, kit.ring[:, 0:SEQ],
             squares=h[:, :, 0:SEQ])

        def residual(x, which, spans, bank_spans, mods):
            def add(dve, j, banks):
                for n, ((t0, w), bank) in enumerate(zip(spans, banks)):
                    at = x[:, bass.ds(j, 1), t0:t0 + w].rearrange("p a n -> p (a n)")
                    g = mods[:, bass.ds(j + which, 1), bank_spans[n]:bank_spans[n] + 1].rearrange("p a n -> p (a n)")
                    ins = dve.scalar_tensor_tensor(out=at, in0=bank, scalar=g, in1=at, op0=ALU.mult, op1=ALU.add)
                return ins
            return add

        def shift(which, lat_only=False):
            return lambda j, n: mods[:, which + j, (1 if lat_only else n):(2 if lat_only else n + 1)]

        def gain(m, lat_only=False):
            return lambda j, n: gains[:, m, j, (1 if lat_only else n):(2 if lat_only else n + 1)]

        modulation_gains(kit, "gains0", mods, gains, cols("n1_0", 8), cols("n2_0", 8))
        with nc.sbuf_tensor("mixed", [P, 8, T2], F32) as y_t:
            y = y_t[:, :, :]
            norm(kit, "norm1_0", x2, KD, T2, gain(0), h, y[:, 0, :], shift=shift(0))
            w_in = matrix(d["w_in0"])
            diff_attention(kit, h, pack2, w_in, d["axial"], y)
            with ExitStack() as rw:
                def rb(name, shape):
                    return rw.enter_context(nc.sbuf_tensor(name, shape, F32))

                f_t = rb("rw_features", [P, 14, W + 2])
                f = f_t[:, :, :]
                f_flat = f.rearrange("p k n -> p (k n)")

                def store(act, j, banks):
                    for n, ((t0, w), bank) in enumerate(zip(spans_of(T2), banks)):
                        ins = act.activation(f_flat[:, bass.ds(j * (W + 2) + (1 + t0 + n), w)], bank, ACT.Copy)
                    return ins

                gemm(kit, "rw_project", w_in[:, :, EVEN_A:EVEN_A + EVEN_B], EVEN_B, h, T2, store,
                     in_place=h_in_place)
                saved, padded = ph.sem("x_saved"), ph.sem("rw_padded")
                with ph as block:
                    @block.sync
                    def _(sp):
                        sp.dma_start(x_saved, x2).then_inc(saved, 16)
                        sp.wait_ge(saved, 16)

                    @block.vector
                    def _(dve):
                        for at in (0, CTX + 1, W + 1):
                            dve.memset(f[:, :, at:at + 1], 0.0)
                kk, b_neg, y_b = (rb(n, [P, 4, W]) for n in ("rw_kk", "rw_b", "rw_y_back"))
                decays, small_cols = rb("rw_decays", [P, 2, 4, 65]), rb("rw_small", [P, 4])
                cum = [h_flat[:, n * 4 * W:(n + 1) * 4 * W].rearrange("p (k n) -> p k n", k=4) for n in range(2)]
                rwkv_prepare(kit, f, [d["w2_f"], d["w2_b"], d["a2"]], pack2, cum, kk[:, :, :], b_neg[:, :, :],
                             small_cols[:, :])
                outs = (lambda at, part: y[:, 4:8, bass.ds(at - part, 64)],
                        lambda at, part: y_b[:, :, bass.ds(at - part, 64)])
                rwkv_scan(kit, f, cum, kk[:, :, :], b_neg[:, :, :], outs,
                          x2.rearrange("p k n -> p (k n)"), decays, small_cols)
                scratch = [h_flat[:, 0:4 * T2].rearrange("p (k n) -> p k n", k=4),
                           h_flat[:, 4 * W:4 * W + 4 * T2].rearrange("p (k n) -> p k n", k=4),
                           kk[:, :, 0:T2]]
                rwkv_finish(kit, f, d["g2"], pack2, y[:, 4:8, :], y_b[:, :, 0:T2], scratch)
                restored = ph.sem("x_restored")
                with ph as block:
                    @block.sync
                    def _(sp):
                        sp.dma_start(x2, x_saved).then_inc(restored, 16)
                        sp.wait_ge(restored, 16)
            gemm(kit, "out0", matrix(d["w_out0"]), D_MODEL, y, T2, residual(x2, 16, spans_of(T2), (0, 1), mods),
                 engine="vector")
        norm(kit, "norm2_0", x2, KD, T2, gain(1), h, kit.ring[:, 0:T2], shift=shift(24))
        mlp(kit, "mlp0", matrix(d["w1_0"]), matrix(d["w2_0"]), h, T2, residual(x2, 40, spans_of(T2), (0, 1), mods),
            in_place=h_in_place)

        mods = mods_of[1]
        modulation_gains(kit, "gains1", mods, gains, cols("n1_1", 8), cols("n2_1", 8))
        with nc.sbuf_tensor("mixed1", [P, 8, SEQ], F32) as y_t:
            y = y_t[:, :, :]
            norm(kit, "norm1_1", x2, KD, T2, gain(0), h, kit.ring[:, 0:T2], shift=shift(0))
            w_in = matrix(d["w_in1"])
            with nc.sbuf_tensor("gate_low", [P, T2], F32) as gd:
                ssm_branch(kit, h, pack2, w_in, y, gd)
                gla_branch(kit, h, gd, pack2, w_in, (d["gk_up_f"], d["gk_up_b"]), y)
            gemm(kit, "out1", matrix(d["w_out1"]), D_MODEL, y, SEQ, residual(x_lat, 16, [(0, SEQ)], (1,), mods),
                 engine="vector")
        h_lat = h[:, :, 0:SEQ]
        norm(kit, "norm2_1", x_lat, KD, SEQ, gain(1, True), h_lat, kit.ring[:, 0:SEQ], shift=shift(24, True))
        mlp(kit, "mlp1", matrix(d["w1_1"]), matrix(d["w2_1"]), h_lat, SEQ, residual(x_lat, 40, [(0, SEQ)], (1,), mods))
        norm(kit, "final_norm", x_lat, KD, SEQ, lambda j, n: cols("final", 1, j), h[:, :, 0:SEQ], kit.ring[:, 0:SEQ])
        return_h(kit, h[:, :, 0:SEQ], d["out"])


def return_h(kit, h, out):
    stored = kit.ph.sem("out_stored")
    with kit.ph as block:
        @block.sync
        def _(sp):
            sp.dma_start(out, h).then_inc(stored, 16)
            sp.wait_ge(stored, 16)


def matrix(w):
    return w.rearrange("(k p) n -> p k n", p=P)


def build(nc, d):
    with ExitStack() as ctx:
        kit = Kit(nc, ctx)
        x2 = ctx.enter_context(nc.sbuf_tensor("x", [P, KD, T2], F32))
        x = x2[:, :, CTX:]
        loaded = kit.ph.sem("x_loaded")
        with kit.ph as block:
            @block.sync
            def _(sp):
                sp.dma_start(kit.consts[:, :], d["consts"]).then_inc(loaded, 16)
                sp.dma_start(x, d["x"]).then_inc(loaded, 16)
                sp.wait_ge(loaded, 32)
        pack_sb, cols, cvec, mods = conditioning(kit, ctx, x2[:, :, :], d)
        with nc.sbuf_tensor("mod_rows", [2, 2, 6 * D_MODEL], F32) as rows:
            fill, finish = modulation(kit, [matrix(d["mod_w0"]), matrix(d["mod_w1"])],
                                      [cols("mod_b0", 48), cols("mod_b1", 48)], cvec, rows, mods)
            bias_dram = nc.dram_tensor("window_bias_dram", (BLOCKS, SWA_HEADS, P, 2 * P), F32, kind="Internal").ap()
            window_bias(kit, d["pos_skewed"], d["pos_column"], d["rel_bias"], bias_dram, fill, finish)
        first_block(kit, x, d, bias_dram)
        second_block(kit, x2[:, :, :], d, pack_sb, cols, mods)


def columns(a, k):
    return np.swapaxes(a.reshape(a.shape[:-1] + (k, P)), -1, -2)


def channel_major(a, k):
    return a.T.reshape(k, P, a.shape[0]).transpose(1, 0, 2)


def layout1(v):
    pos = v["positions"][0]
    padded = np.concatenate([np.zeros(P, pos.dtype), pos])
    taps = v["w_dw"][:, :, 0, :].reshape(DEPTH, TAPS, 4, P).transpose(0, 3, 2, 1).reshape(DEPTH, P, 4 * TAPS)
    pack = [columns(v["g_mix"], 8), columns(v["g_mlp"], 8), columns(v["g_q_norm"], 2), columns(v["g_kv_norm"], 1),
            columns(v["b_dw"], 4), columns(v["g_conv_ln"], 4), columns(v["b_conv_ln"], 4), taps,
            np.broadcast_to(v["swa_sinks"][:, None, :], (DEPTH, P, SWA_HEADS))]
    windows = np.stack([padded[q + 1:q + 1 + P] for q in range(SEQ)])
    return {
        "consts": CONSTS, "axial": AXIAL, "x": channel_major(v["x"][0], KD),
        "pos_skewed": windows.reshape(BLOCKS, P, P).transpose(1, 0, 2).reshape(P, SEQ),
        "pos_column": pos.reshape(BLOCKS, P).T,
        "positions": np.broadcast_to(pos, (32, SEQ)),
        "rel_bias": np.broadcast_to(v["rel_bias"], (P,) + v["rel_bias"].shape),
        "pack1": np.concatenate(pack, -1),
        "w_in": v["w_in"], "w_branch": v["w_branch"].reshape(DEPTH, 3 * 512, D_MODEL),
        "w_out": v["w_out"], "w_up": v["w_up"], "w_down": v["w_down"],
        "w_q_up": v["w_q_up"], "w_kv_up": v["w_kv_up"],
    }


def layout2(v):
    g = {n[:-2]: a for n, a in v.items() if n.endswith("_2")}

    def rows(a):
        return np.broadcast_to(a, (P,) + a.shape)

    lam = np.zeros((P, 4), np.float32)
    for n, name in enumerate(("lam_q1", "lam_k1", "lam_q2", "lam_k2")):
        lam[:64, n] = g[f"l0_{name}"]
    c = np.stack([columns(g["c_ctx"], KD), columns(g["c"][0], KD)], -1).reshape(P, 16)
    col = {
        "mod_b0": columns(g["l0_mod_b"], 48), "mod_b1": columns(g["l1_mod_b"], 48),
        "n1_0": columns(g["l0_norm1"], 8), "n2_0": columns(g["l0_norm2"], 8),
        "n1_1": columns(g["l1_norm1"], 8), "n2_1": columns(g["l1_norm2"], 8),
        "final": columns(g["final_norm"], 8), "g_final": columns(v["g_final"], 8), "c": c, "lam": lam,
        "subln": columns(g["l0_subln"], 1), "mu": columns(g["l0_mu"], 14),
        "w0_f": columns(g["l0_w0_f"], 4), "w0_b": columns(g["l0_w0_b"], 4), "a0": columns(g["l0_a0"], 4),
        "k_k": columns(g["l0_k_k"], 4), "k_a": columns(g["l0_k_a"], 4), "r_k": columns(g["l0_r_k"], 4),
        "lnx_w": columns(g["l0_lnx_w"], 4), "lnx_b": columns(g["l0_lnx_b"], 4),
        "conv_w": g["l1_conv_w"].reshape(5, 8, P).transpose(2, 1, 0).reshape(P, 40),
        "conv_b": columns(g["l1_conv_b"], 8),
        "dt_bias": rows(np.concatenate([g["l1_dt_bias_f"], g["l1_dt_bias_b"]])),
        "a_log": rows(np.concatenate([g["l1_a_log_f"], g["l1_a_log_b"]])),
        "d_skip": columns(np.repeat(g["l1_d_skip"], 64), 4), "ssm_norm": columns(g["l1_ssm_norm"], 4),
        "gk_b": np.concatenate([columns(g["l1_gk_b_f"], 2), columns(g["l1_gk_b_b"], 2)], 1),
        "gla_norm": columns(g["l1_gla_norm"], 1),
    }
    out = {"pack2": np.concatenate([col[n] for n, _ in PACK2], 1), "ctx": channel_major(g["ctx"][0], KD)}
    for name, source in (("mod_w0", "l0_mod_w"), ("mod_w1", "l1_mod_w"), ("w_in0", "l0_w_in"), ("w_in1", "l1_w_in"),
                         ("w_out0", "l0_w_out"), ("w_out1", "l1_w_out"), ("w1_0", "l0_mlp_w1"), ("w2_0", "l0_mlp_w2"),
                         ("w1_1", "l1_mlp_w1"), ("w2_1", "l1_mlp_w2"), ("w2_f", "l0_w2_f"), ("w2_b", "l0_w2_b"),
                         ("a2", "l0_a2"), ("g2", "l0_g2"), ("gk_up_f", "l1_gk_up_f"), ("gk_up_b", "l1_gk_up_b")):
        out[name] = g[source]
    return out


def kernel(**inputs):
    import concourse.bacc as bacc
    from concourse.bass_utils import run_bass_kernel_spmd

    nc = bacc.Bacc("TRN2", target_bir_lowering=False, num_devices=1)
    v = {k: np.asarray(a) for k, a in inputs.items()}
    arrays, d = {}, {}
    for name, a in {**layout1(v), **layout2(v)}.items():
        a = np.ascontiguousarray(a)
        arrays[f"in_{name}"] = a
        d[name] = nc.dram_tensor(f"in_{name}", a.shape, mybir.dt.from_np(a.dtype), kind="ExternalInput").ap()
    d["out"] = nc.dram_tensor("out", (P, KD, SEQ), F32, kind="ExternalOutput").ap()
    build(nc, d)
    r = run_bass_kernel_spmd(nc, [arrays], core_ids=[0])
    return r.results[0]["out"].transpose(1, 0, 2).reshape(D_MODEL, SEQ).T[None]
```
